# Optimizing a Trainium2 kernel written in Bass

```python
import jax, jax.numpy as jnp
from jax import lax
import numpy as np

D_MODEL = 2048
BATCH = 1
SEQ = 256
DEPTH = 1

MIX_WIDTH = D_MODEL
ATTN_HEAD_DIM = 128
ATTN_WIDTH = MIX_WIDTH // 2
ATTN_HEADS = ATTN_WIDTH // ATTN_HEAD_DIM
HGRN_HEAD_DIM = 128
HGRN_WIDTH = MIX_WIDTH - ATTN_WIDTH
HGRN_HEADS = HGRN_WIDTH // HGRN_HEAD_DIM
IN_SPLITS = [ATTN_WIDTH, ATTN_WIDTH, ATTN_WIDTH, HGRN_WIDTH, HGRN_WIDTH, HGRN_WIDTH, HGRN_WIDTH]
IN_WIDTH = sum(IN_SPLITS)

MOBA_BLOCK = 256
MOBA_TOPK = 3
MOBA_QCHUNK = 64
HGRN_CHUNK = 64
PEER_HEADS = 8
PEER_N_KEYS = 128
PEER_N_EXPERTS = PEER_N_KEYS * PEER_N_KEYS
PEER_QUERY_DIM = 256
PEER_SUB_DIM = PEER_QUERY_DIM // 2
PEER_TOPK = 16
PEER_TOKEN_CHUNK = 128
PLE_DIM = 256
EPS = 1e-6

kernel_name = "hybrid_moba_hgrn2_peer_block"

def rms_norm(x, gain):
    xf = x.astype(jnp.float32)
    y = xf * lax.rsqrt(jnp.mean(xf * xf, axis=-1, keepdims=True) + EPS)
    return (y * gain.astype(jnp.float32)).astype(x.dtype)

def moba_attention(q, k, v):
    B, S, H, Dh = q.shape
    L = MOBA_BLOCK
    nb = -(-S // L)
    S_pad = nb * L
    pad = ((0, 0), (0, S_pad - S), (0, 0), (0, 0))
    q = jnp.pad(q, pad)
    k = jnp.pad(k, pad)
    v = jnp.pad(v, pad)
    kb = k.reshape(B, nb, L, H, Dh).transpose(0, 3, 1, 2, 4)
    vb = v.reshape(B, nb, L, H, Dh).transpose(0, 3, 1, 2, 4)
    qh = q.transpose(0, 2, 1, 3)
    k_mean = jnp.mean(kb.astype(jnp.float32), axis=3)
    gate = jnp.einsum('bhtd,bhnd->bhtn', qh.astype(jnp.float32), k_mean)
    q_blk = jnp.arange(S_pad) // L
    fully_past = jnp.arange(nb)[None, :] < q_blk[:, None]
    gate = jnp.where(fully_past, gate, -jnp.inf)
    k_sel = min(MOBA_TOPK, nb)
    _, sel = lax.top_k(gate, k_sel)
    sel_valid = sel < q_blk[:, None]
    scale = Dh ** -0.5
    Q = MOBA_QCHUNK
    n_chunks = S_pad // Q
    b_idx = jnp.arange(B)[:, None, None, None]
    h_idx = jnp.arange(H)[None, :, None, None]

    def chunk(c):
        start = c * Q
        qc = lax.dynamic_slice_in_dim(qh, start, Q, axis=2)
        sc = lax.dynamic_slice_in_dim(sel, start, Q, axis=2)
        vc = lax.dynamic_slice_in_dim(sel_valid, start, Q, axis=2)
        kg = kb[b_idx, h_idx, sc]
        vg = vb[b_idx, h_idx, sc]
        own = start // L
        k_own = lax.dynamic_index_in_dim(kb, own, axis=2, keepdims=False)
        v_own = lax.dynamic_index_in_dim(vb, own, axis=2, keepdims=False)
        s_sel = jnp.einsum('bhqd,bhqnld->bhqnl', qc, kg).astype(jnp.float32) * scale
        s_sel = jnp.where(vc[..., None], s_sel, -jnp.inf).reshape(B, H, Q, k_sel * L)
        s_own = jnp.einsum('bhqd,bhld->bhql', qc, k_own).astype(jnp.float32) * scale
        q_pos = start + jnp.arange(Q)
        k_pos = own * L + jnp.arange(L)
        s_own = jnp.where(k_pos[None, :] <= q_pos[:, None], s_own, -jnp.inf)
        probs = jax.nn.softmax(jnp.concatenate([s_sel, s_own], axis=-1), axis=-1).astype(q.dtype)
        p_sel = probs[..., :k_sel * L].reshape(B, H, Q, k_sel, L)
        p_own = probs[..., k_sel * L:]
        return (jnp.einsum('bhqnl,bhqnld->bhqd', p_sel, vg)
                + jnp.einsum('bhql,bhld->bhqd', p_own, v_own))

    out = lax.map(chunk, jnp.arange(n_chunks))
    out = out.transpose(1, 0, 3, 2, 4).reshape(B, S_pad, H * Dh)
    return out[:, :S]

def hgrn2(q, f_logit, i_in, g, lb, out_gain):
    B, S, H, K = q.shape
    dtype = q.dtype
    lbh = lb.astype(jnp.float32).reshape(H, K)
    f = lbh + (1.0 - lbh) * jax.nn.sigmoid(f_logit.astype(jnp.float32))
    log_f = jnp.log(f)
    kk = 1.0 - f
    qq = jax.nn.silu(q.astype(jnp.float32))
    vv = i_in.astype(jnp.float32)
    C = HGRN_CHUNK
    n = S // C

    def to_chunks(a):
        return a.reshape(B, n, C, H, K).transpose(1, 0, 3, 2, 4)

    qs, ks, vs = to_chunks(qq), to_chunks(kk), to_chunks(vv)
    bs = jnp.cumsum(to_chunks(log_f), axis=3)
    causal = jnp.tril(jnp.ones((C, C), dtype=bool))

    def step(state, inp):
        qc, kc, vc, bc = inp
        o_inter = jnp.einsum('bhck,bhkv->bhcv', qc * jnp.exp(bc), state)
        diff = bc[:, :, :, None, :] - bc[:, :, None, :, :]
        decay = jnp.exp(jnp.where(causal[None, None, :, :, None], diff, -jnp.inf))
        attn = jnp.einsum('bhtk,bhsk,bhtsk->bhts', qc, kc, decay)
        o_intra = jnp.einsum('bhts,bhsv->bhtv', attn, vc)
        b_last = bc[:, :, -1, :]
        k_dec = kc * jnp.exp(b_last[:, :, None, :] - bc)
        new_state = (jnp.exp(b_last)[..., None] * state
                     + jnp.einsum('bhsk,bhsv->bhkv', k_dec, vc))
        return new_state, o_inter + o_intra

    state0 = jnp.zeros((B, H, K, K), jnp.float32)
    _, o = lax.scan(step, state0, (qs, ks, vs, bs))
    o = o.transpose(1, 0, 3, 2, 4).reshape(B, S, H, K)
    o = rms_norm(o, out_gain.reshape(H, K))
    o = o * jax.nn.silu(g.astype(jnp.float32))
    return o.reshape(B, S, H * K).astype(dtype)

def peer(h, w_query, sub_keys, expert_down, expert_up):
    B, S, D = h.shape
    kt = PEER_TOPK
    qry = (h @ w_query).reshape(B, S, PEER_HEADS, 2, PEER_SUB_DIM)
    scores = jnp.einsum('bshpd,hpnd->bshpn', qry, sub_keys).astype(jnp.float32)
    top_s, top_i = lax.top_k(scores, kt)
    cand_s = top_s[..., 0, :, None] + top_s[..., 1, None, :]
    cand_i = top_i[..., 0, :, None] * PEER_N_KEYS + top_i[..., 1, None, :]
    best_s, best_pos = lax.top_k(cand_s.reshape(B, S, PEER_HEADS, kt * kt), kt)
    expert_idx = jnp.take_along_axis(cand_i.reshape(B, S, PEER_HEADS, kt * kt), best_pos, axis=-1)
    gates = jax.nn.softmax(best_s, axis=-1).astype(h.dtype)
    T = B * S
    c = PEER_TOKEN_CHUNK
    hf = h.reshape(T // c, c, D)
    idx = expert_idx.reshape(T // c, c, PEER_HEADS * kt)
    gf = gates.reshape(T // c, c, PEER_HEADS * kt)

    def step(args):
        hc, ic, gc = args
        u = expert_down[ic]
        act = jax.nn.gelu(jnp.einsum('cd,ced->ce', hc, u), approximate=False)
        v = expert_up[ic]
        return jnp.einsum('ce,ced->cd', act * gc, v)

    out = lax.map(step, (hf, idx, gf))
    return out.reshape(B, S, D)

def setup_inputs(seed: int = 0) -> dict:
    key = jax.random.key(seed)
    ks = jax.random.split(key, 16)
    f32 = jnp.float32

    def nrm(k, shape, scale):
        return jax.random.normal(k, shape, f32) * scale

    def gain(k, shape):
        return 1.0 + 0.02 * jax.random.normal(k, shape, f32)

    return {
        "x": nrm(ks[0], (BATCH, SEQ, D_MODEL), 1.0),
        "p": nrm(ks[1], (DEPTH, BATCH, SEQ, PLE_DIM), 1.0),
        "norm_mix": gain(ks[2], (DEPTH, D_MODEL)),
        "w_in": nrm(ks[3], (DEPTH, D_MODEL, IN_WIDTH), D_MODEL ** -0.5),
        "lb_logits": nrm(ks[4], (DEPTH + 1, HGRN_WIDTH), 0.5),
        "hgrn_norm": gain(ks[5], (DEPTH, HGRN_WIDTH)),
        "w_out": nrm(ks[6], (DEPTH, MIX_WIDTH, D_MODEL), MIX_WIDTH ** -0.5),
        "norm_ffn": gain(ks[7], (DEPTH, D_MODEL)),
        "peer_query": nrm(ks[8], (DEPTH, D_MODEL, PEER_HEADS * PEER_QUERY_DIM), D_MODEL ** -0.5),
        "peer_sub_keys": nrm(ks[9], (DEPTH, PEER_HEADS, 2, PEER_N_KEYS, PEER_SUB_DIM), PEER_SUB_DIM ** -0.5),
        "peer_down": nrm(ks[10], (DEPTH, PEER_N_EXPERTS, D_MODEL), D_MODEL ** -0.5),
        "peer_up": nrm(ks[11], (DEPTH, PEER_N_EXPERTS, D_MODEL), PEER_HEADS ** -0.5),
        "norm_ple": gain(ks[12], (DEPTH, D_MODEL)),
        "w_ple": nrm(ks[13], (DEPTH, PLE_DIM, D_MODEL), PLE_DIM ** -0.5),
        "w_ple_gate": nrm(ks[14], (DEPTH, D_MODEL, D_MODEL), D_MODEL ** -0.5),
        "norm_final": gain(ks[15], (D_MODEL,)),
    }

def reference(x, p, norm_mix, w_in, lb_logits, hgrn_norm, w_out, norm_ffn, peer_query,
              peer_sub_keys, peer_down, peer_up, norm_ple, w_ple, w_ple_gate, norm_final):
    B, S, D = x.shape
    lb_all = jnp.cumsum(jax.nn.softmax(lb_logits.astype(jnp.float32), axis=0), axis=0)
    split_points = list(np.cumsum(IN_SPLITS)[:-1])
    h = x
    for layer in range(DEPTH):
        hn = rms_norm(h, norm_mix[layer])
        proj = hn @ w_in[layer]
        aq, ak, av, gq, gf, gi, gg = jnp.split(proj, split_points, axis=-1)
        a_shape = (B, S, ATTN_HEADS, ATTN_HEAD_DIM)
        g_shape = (B, S, HGRN_HEADS, HGRN_HEAD_DIM)
        attn_out = moba_attention(aq.reshape(a_shape), ak.reshape(a_shape), av.reshape(a_shape))
        rec_out = hgrn2(gq.reshape(g_shape), gf.reshape(g_shape), gi.reshape(g_shape),
                        gg.reshape(g_shape), lb_all[layer], hgrn_norm[layer])
        mixed = jnp.concatenate([attn_out, rec_out], axis=-1)
        h = h + mixed @ w_out[layer]
        h = h + peer(rms_norm(h, norm_ffn[layer]), peer_query[layer], peer_sub_keys[layer],
                     peer_down[layer], peer_up[layer])
        ple = p[layer] @ w_ple[layer]
        ple_gate = jax.nn.sigmoid(rms_norm(h, norm_ple[layer]) @ w_ple_gate[layer])
        h = h + ple_gate * ple
    return rms_norm(h, norm_final)


_drawn_inputs = setup_inputs


def setup_inputs(seed=0):
    import zlib

    import numpy as np

    out = dict(_drawn_inputs(seed))
    spreads = {}
    factors = {'norm_mix': 2.774,
     'hgrn_norm': 10.275,
     'norm_ple': 200.0,
     'norm_final': 20.719,
     'norm_ffn': 21.677}
    for name, (base, spread) in spreads.items():
        noise = np.random.default_rng([zlib.crc32(name.encode()), seed]).standard_normal(out[name].shape)
        drawn = base * np.exp(spread * noise) if base else spread * noise
        out[name] = __import__('jax').numpy.asarray(drawn.astype(out[name].dtype))
    for name, factor in factors.items():
        out[name] = (out[name] * factor).astype(out[name].dtype)
    return out
```

```python
from contextlib import ExitStack

import numpy as np

import concourse.bass as bass
from concourse import mybir

F32 = mybir.dt.float32
F32R = mybir.dt.float32r
U32 = mybir.dt.uint32
ALU = mybir.AluOpType
ACT = mybir.ActivationFunctionType
AX = mybir.AxisListType.X

P = 128
D = 2048
S = 256
TT = S // P
KC = D // P
HEADS = 8
HW = HEADS * P
GRP = 512
TILE = 1024
RAW = 4
HI = 4
LO = 2
COLT = KC * P // TILE
ROUTE_TRIPS = 3
GRPT = KC * GRP // TILE
KPC = TILE // P
KPG = TILE // GRP
HALVES = [128, 64, 32, 16, 8, 4, 2, 1]
NL = len(HALVES)
PH = 8
NK = 128
TOP = 16
PLE = 256
PK = PLE // P
EPS = 1e-6
SCALE = float(P) ** -0.5
NEG = -3.0e38
MISC = 2944
TINY = 2.0 ** -64

A_COLS, B_GRPS, D_COLS, E_GRPS, F_COLS, W_GRPS = 16, 6, 16, D // GRP, 2 * PH, D // GRP
A0 = 0
B0 = A0 + A_COLS * COLT
D0 = B0 + B_GRPS * GRPT
E0 = D0 + D_COLS * COLT
F0 = E0 + E_GRPS * GRPT
G0 = F0 + F_COLS * COLT
U0 = G0 + NK * COLT
W0 = U0 + NK * D // TILE
CA, CD, CF, CG = 0, A_COLS, A_COLS + D_COLS, A_COLS + D_COLS + F_COLS
GB, GE, GW = 0, B_GRPS, B_GRPS + E_GRPS


def program(nc, x, win_t, win_n, wout, wq, down, up, wgate, gains, lbl, gain_h, gain_f, skt, pt, wple,
            consts, mix_consts, level_masks, out):
    with ExitStack() as ctx:
        def sb(name, shape, dt=F32):
            return ctx.enter_context(nc.sbuf_tensor(name, shape, dt))

        def sem(name):
            return ctx.enter_context(nc.semaphore(name))

        h_spill = nc.dram_tensor("h_spill", [P, TT * D], F32, kind="Internal").ap()

        arena = sb("arena", [P, NK * S])
        raw = sb("raw", [P, RAW, TILE])
        whi = sb("whi", [P, HI, TILE], F32R)
        wlo = sb("wlo", [P, LO, TILE], F32R)
        xh = sb("xh", [P, KC, S], F32R)
        xl = sb("xl", [P, KC, S], F32R)
        cst = sb("cst", [P, 2 * P])
        gain = sb("gain", [P, 3, KC])
        ss = sb("ss", [P, 32])
        rstd = sb("rstd", [P, 32])
        half = sb("half", [P, 16])
        lb = sb("lb", [P, 8, HEADS])
        small = sb("small", [P, 8])
        ch = sb("ch", [P, 2, S], F32R)
        cl = sb("cl", [P, 2, S], F32R)
        misc = sb("misc", [P, MISC])

        def view(of, base, shape):
            v = of[:, base:base + int(np.prod(shape))]
            names = "abc"[:len(shape)]
            return v if len(shape) == 1 else v.rearrange(
                f"p ({' '.join(names)}) -> p {' '.join(names)}", **dict(zip(names, shape)))

        ident, iota = cst[:, 0:P], cst[:, P:2 * P]

        at = {"arena": 0, "misc": 0}

        def take(*shape, of="arena"):
            v = view(arena if of == "arena" else misc, at[of], shape)
            at[of] += int(np.prod(shape))
            return v

        h = take(TT, D)
        hn = view(arena, at["arena"], (TT, D))
        sf = take(HEADS, S)
        qq = take(HEADS, S)
        take(B_GRPS // 2, TT, HW)
        tok = arena[:, at["arena"] - B_GRPS // 2 * TT * HW:at["arena"]]

        def tokens(which):
            return tok[:, which * TT * HW:(which + 1) * TT * HW].rearrange("p (t c) -> p t c", t=TT)

        gi, gs, va = tokens(0), tokens(1), tokens(2)
        orec = take(TT, HW)
        grow = orec[:, 0, :]
        QL_AT = at["arena"]
        QL, KL = take(2 * NL, S), take(2 * NL, S)
        E = take(NL - 1, S)
        masks = take(NL, P)
        amask = take(NL, P)
        a00, a01, a11 = take(P), take(P), take(P)
        mix_c = take(3 * P + S)
        cmask, ones = mix_c[:, 0:3 * P], mix_c[:, 3 * P:]
        qk = take(4, S)
        att = take(HEADS, S)
        assert at["arena"] <= NK * S
        fk = take(4, S, of="misc")
        kk = take(2, S, of="misc")
        pr = take(3 * P, of="misc")
        pT = take(3 * P, of="misc")
        vh = take(2, P, of="misc")
        junk = take(2, P, of="misc")
        assert at["misc"] <= MISC
        sk = view(arena, 8192, (2 * PH, NK))
        qT = view(arena, 10240, (2 * PH, S))
        SC_AT = NK * S - TT * 2 * PH * NK
        sc = view(arena, SC_AT, (TT * 2 * PH, NK))
        at["misc"] = 0
        i1, i2, best, gate = (take(TT * PH, TOP, of="misc") for _ in range(4))
        R = at["misc"]
        sg, sg2 = take(2, NK, of="misc"), take(2, NK, of="misc")
        top, tixu, tix = take(2, TOP, of="misc"), take(2, TOP, of="misc").bitcast(U32), take(2, TOP, of="misc")
        cand, cand2 = take(TOP, TOP, of="misc"), take(TOP, TOP, of="misc")
        bst, posu = take(TOP, of="misc"), take(TOP, of="misc").bitcast(U32)
        abu, ab = take(2, TOP, of="misc").bitcast(U32), take(2, TOP, of="misc")
        oh = take(2, TOP, TOP, of="misc")
        isel = take(2, TOP, of="misc")
        gsum = take(TT * PH, of="misc")
        assert at["misc"] <= MISC
        at["misc"] = R
        slotT = take(3, S, of="misc")
        gateR = take(2 * 4, P, of="misc")
        oneL = view(xh.rearrange("p a b -> p (a b)"), 0, (2 * 4, P))
        assert at["misc"] <= MISC
        coef = view(arena, 0, (NK, S))
        coef_t = arena[:, :].rearrange("p (e t) -> p t e", t=S)
        ple_w = view(arena, 8192, (PK, D))
        ple_p = view(arena, 12288, (PK, S))
        gf_row = view(arena, 12800, (D,))
        sgate = view(arena, 16384, (2 * TT, GRP))
        ple_m = view(arena, 18432, (2 * TT, GRP))
        orow = view(arena, 20480, (TT, D))

        ps = ctx.enter_context(nc.psum_tensor("ps", [P, 8, 512], F32))

        def col_ps(bank):
            return ps[:, bank, 0:S]

        const_in = sem("const_in")
        mask_in = sem("mask_in")
        h_in = [sem(f"h_in{t}") for t in range(TT)]
        raw_in = [sem(f"raw_in{i}") for i in range(RAW)]
        hi_ready, lo_ready, tile_done = sem("hi_ready"), sem("lo_ready"), sem("tile_done")
        col_free = sem("col_free")
        grp_free = sem("grp_free")
        lb_step, lb_act = sem("lb_step"), sem("lb_act")
        NORMS = ["mix", "ffn", "ple"]
        n_sq, n_rs, n_row, n_tr, n_xh, n_xl = (
            [sem(f"n_{what}_{n}") for n in NORMS] for what in ("sq", "rs", "row", "tr", "xh", "xl"))
        pool_step, zeroed = sem("pool_step"), sem("zeroed")
        silu_g, gain_g = sem("silu_g"), sem("gain_g")
        f_ready, logf_ready, d_ready, e_ready, qk_ready = (
            sem(n) for n in ("f_ready", "logf_ready", "d_ready", "e_ready", "qk_ready"))
        pre_step, soft_step, mid_step = sem("pre_step"), sem("soft_step"), sem("mid_step")
        s_full, min_ready, exp_ready, p_ready = (sem(n) for n in ("s_full", "min_ready", "exp_ready", "p_ready"))
        a_full, a_ready, ax_ready = sem("a_full"), sem("a_ready"), sem("ax_ready")
        pt_full, pt_sb, v_ready = sem("pt_full"), sem("pt_sb"), sem("v_ready")
        o_full, att_sb, rec_sb = sem("o_full"), sem("att_sb"), sem("rec_sb")
        att_hi, att_lo = sem("att_hi"), sem("att_lo")
        r_rs, r_row, r_tr, r_hi, r_lo = (sem(f"r_{n}") for n in ("rs", "row", "tr", "hi", "lo"))
        spilled, sk_in, sc_full, sc_sb = sem("spilled"), sem("sk_in"), sem("sc_full"), sem("sc_sb")
        rt_step, routed, gexp, g_step, gates = (sem(n) for n in ("rt_step", "routed", "gexp", "g_step", "gates"))
        it_full, it_sb = sem("it_full"), sem("it_sb")
        oh_ready, gm_full, gm_mul = sem("oh_ready"), sem("gm_full"), sem("gm_mul")
        c_hi, c_lo = sem("c_hi"), sem("c_lo")
        h_back, h_up, ple_in = sem("h_back"), sem("h_up"), sem("ple_in")
        w_sig, w_add = sem("w_sig"), sem("w_add")
        f_sq, f_rs, f_row, stored = sem("f_sq"), sem("f_rs"), sem("f_row"), sem("stored")

        block = ctx.enter_context(nc.Block())

        @block.sync
        def _(sp):
            for t in range(TT):
                sp.dma_start(h[:, t, :], x[t * P:(t + 1) * P, :]).then_inc(h_in[t], 16)
            sp.dma_start(cst[:], consts).then_inc(const_in, 16)
            sp.dma_start(gain[:], gains).then_inc(const_in, 16)
            sp.dma_start(lb[:, 0:2, :], lbl).then_inc(const_in, 16)

            def load(src, s, split):
                if split is not None:
                    sp.wait_ge(lo_ready, split)
                sp.dma_start(raw[:, s, :], src).then_inc(raw_in[s], 16)

            def stream(src, base, tiles, first=0):
                with sp.Fori(0, tiles // RAW) as i:
                    for s in range(RAW):
                        load(src[RAW * i + (first + s)], s, RAW * i + (base + s - RAW + 1))

            for s in range(RAW):
                load(win_t[s], s, None)
            sp.dma_start(masks.rearrange("p a b -> p (a b)"), level_masks).then_inc(mask_in, 16)
            sp.dma_start(grow, gain_h.partition_broadcast(P)).then_inc(mask_in, 16)
            sp.dma_start(mix_c, mix_consts).then_inc(mask_in, 16)
            with sp.Fori(1, A_COLS * COLT // RAW) as i:
                for s in range(RAW):
                    load(win_t[RAW * i + s], s, RAW * i + (s - RAW + 1))
            stream(win_n, B0, D0 - B0)
            stream(win_t, D0, E0 - D0, A_COLS * COLT)
            stream(wout, E0, F0 - E0)
            sp.wait_ge(grp_free, TT * GW)
            sp.dma_start(sk.rearrange("p a b -> p (a b)"), skt).then_inc(sk_in, 16)
            sp.dma_start(h_spill, h.rearrange("p a b -> p (a b)")).then_inc(spilled, 16)
            stream(wq, F0, G0 - F0)
            stream(down, G0, U0 - G0)
            with sp.Fori(0, NK * COLT // RAW) as i:
                for s in range(RAW):
                    load(up[2 * i + s // 2, :, (s % 2) * TILE:(s % 2 + 1) * TILE], s,
                         RAW * i + (U0 + s - RAW + 1))
            sp.wait_ge(c_lo, NK)
            sp.dma_start(h.rearrange("p a b -> p (a b)"), h_spill).then_inc(h_back, 16)
            sp.dma_start(ple_w.rearrange("p a b -> p (a b)"), wple).then_inc(ple_in, 16)
            sp.dma_start(ple_p.rearrange("p a b -> p (a b)"), pt).then_inc(ple_in, 16)
            sp.dma_start(gf_row, gain_f.partition_broadcast(P)).then_inc(ple_in, 16)
            stream(wgate, W0, W_GRPS * GRPT)
            for t in range(TT):
                sp.wait_ge(f_row, t + 1)
                sp.dma_start(out[t * P:(t + 1) * P, :], orow[:, t, :]).then_inc(stored, 16)
            sp.wait_ge(stored, 16 * TT)

        @block.gpsimd
        def _(pool):
            steps = 0

            def power(first, width, count, ready, need, done):
                nonlocal steps
                v = ss[:, first:first + width]
                pool.wait_ge(ready, need)
                pool.tensor_scalar(v, v, 1.0 / count, EPS, ALU.mult, ALU.add).then_inc(pool_step, 1)
                steps += 1
                pool.wait_ge(pool_step, steps)
                pool.tensor_tensor(rstd[:, first:first + width], v, half[:, 0:width], ALU.pow).then_inc(done, 1)

            steps += 1
            pool.memset(half[:], -0.5).then_inc(pool_step, 1)
            pool.memset(arena[:, QL_AT:QL_AT + 4 * NL * S], 0.0).then_inc(zeroed, 1)
            power(0, TT, D, n_sq[0], TT, n_rs[0])
            pool.wait_ge(silu_g, 1)
            pool.wait_ge(mask_in, 48)
            for t in range(TT):
                pool.tensor_tensor(gs[:, t, :], gs[:, t, :], grow, ALU.mult).then_inc(gain_g, 1)
            pool.wait_ge(grp_free, TT * B_GRPS)
            pool.tensor_copy(vh, va[:, :, 0:P]).then_inc(v_ready, 1)
            with pool.Fori(1, HEADS) as i:
                pool.wait_ge(o_full, i)
                pool.tensor_copy(vh, va[:, :, bass.DynSlice(i * P, P)]).then_inc(v_ready, 1)
            power(8, TT * HEADS, P, rec_sb, 2 * HEADS, r_rs)
            power(2, TT, D, n_sq[1], TT, n_rs[1])
            power(4, TT, D, n_sq[2], TT, n_rs[2])
            power(24, TT, D, f_sq, TT, f_rs)

        @block.scalar
        def _(act):
            def hi(i, base, s):
                act.wait_ge(raw_in[s % RAW], 16 * i + 16 * ((base + s) // RAW + 1))
                act.wait_ge(tile_done, RAW * i + (base + s + 1))
                act.copy(whi[:, s % HI, :], raw[:, s % RAW, :]).then_inc(hi_ready, 1)

            def norm(k):
                for t in range(TT):
                    if k == 0:
                        act.wait_ge(h_in[t], 16)
                    act.activation(hn[:, t, :], h[:, t, :], ACT.Square,
                                   accum_out=ss[:, 2 * k + t:2 * k + t + 1]).then_inc(n_sq[k], 1)
                for b in range(KC // 2):
                    act.wait_ge(n_tr[k], b + 1)
                    for c in (2 * b, 2 * b + 1):
                        m = act.activation(xh[:, c, :], ps[:, b, (c % 2) * S:(c % 2 + 1) * S], ACT.Copy,
                                           scale=gain[:, k, c:c + 1])
                    m.then_inc(n_xh[k], 1)

            def col_out(dst, bank, func, tiles):
                act.wait_ge(tile_done, tiles + HI)
                act.activation(dst, col_ps(bank), func).then_inc(col_free, 1)

            def cols(base, trips, dst, func, before):
                def body(i, prev):
                    for b in range(2):
                        hi(i, base, 2 * b)
                        hi(i, base, 2 * b + 1)
                        if prev is not None:
                            col_out(prev[0](i, b), b, prev[1], RAW * i + (base - RAW + COLT * (b + 1)))

                body(0, before)
                if trips > 1:
                    with act.Fori(1, trips) as i:
                        body(i, (lambda i, b: dst(2 * i + (b - 2)), func))

            def cols_end(dst, func, last, tiles):
                for b in range(2):
                    col_out(dst(last - 1 + b), b, func, tiles - COLT * (1 - b))

            act.wait_ge(lb_step, 3)
            act.activation(lb[:, 5:7, :], lb[:, 3:5, :], ACT.Exp).then_inc(lb_act, 1)
            norm(0)

            NF = HEADS // 2
            cols(A0, NF, lambda j: sf[:, j, :], ACT.Sigmoid, None)
            cols(A0 + NF * RAW, NF, lambda j: qq[:, j, :], ACT.Silu,
                 (lambda i, b: sf[:, HEADS - 2 + b, :], ACT.Sigmoid))
            cols_end(lambda j: qq[:, j, :], ACT.Silu, HEADS - 1, B0)

            def grp_out(pair, j, tiles):
                act.wait_ge(tile_done, tiles + HI)
                for t in range(TT):
                    act.copy(tok[:, bass.DynSlice(pair * (TT * HW) + t * HW + j * GRP, GRP)],
                             ps[:, 2 + 2 * j + t, :]).then_inc(grp_free, 1)

            def b_body(i, first):
                for j in range(2):
                    for s in range(GRPT):
                        hi(4 * i, B0, j * GRPT + s)
                        if s == HI - 1 and not (first and j == 0):
                            grp_out(i - 1 + j, 1 - j, 2 * GRPT * i + (B0 + j * GRPT))

            b_body(0, True)
            with act.Fori(1, B_GRPS // 2) as i:
                b_body(i, False)
            grp_out(B_GRPS // 2 - 1, 1, D0)
            act.wait_ge(grp_free, 2 * B_GRPS)
            act.activation(gs, gs, ACT.Silu).then_inc(silu_g, 1)

            def d_body(i, u, first=False, last=False):
                hd = 2 * i + u
                if not last:
                    hi(2 * i, D0, 4 * u)
                if not first:
                    act.wait_ge(tile_done, 2 * COLT * hd + (D0 + HI))
                    act.copy(qk[:, 2 * (1 - u) + 1, :], col_ps(1)).then_inc(col_free, 1)
                if not last:
                    act.wait_ge(f_ready, hd + 1)
                    act.activation(fk[:, 2, :], fk[:, 1, :], ACT.Ln).then_inc(logf_ready, 1)
                    hi(2 * i, D0, 4 * u + 1)
                if not first:
                    act.wait_ge(min_ready, hd)
                    for t in range(TT):
                        r = slice(0, P) if t == 0 else slice(P, 3 * P)
                        act.activation(pr[:, r], pr[:, r], ACT.Exp, scale=-1.0, bias=small[:, t:t + 1],
                                       accum_out=small[:, 2 + t:3 + t]).then_inc(exp_ready, 1)
                    act.wait_ge(a_full, 2 * hd - 1)
                    act.copy(a01, ps[:, 7, 3 * P:4 * P]).then_inc(ax_ready, 1)
                if not last:
                    hi(2 * i, D0, 4 * u + 2)
                    act.wait_ge(tile_done, 2 * COLT * hd + (D0 + COLT + HI))
                    act.copy(qk[:, 2 * u, :], col_ps(0)).then_inc(col_free, 1)
                    act.wait_ge(d_ready, hd + 1)
                    act.activation(E, E, ACT.Exp).then_inc(e_ready, 1)
                    hi(2 * i, D0, 4 * u + 3)
                if not first:
                    act.wait_ge(pt_full, hd)
                    act.copy(pT, ps[:, 7, 0:3 * P]).then_inc(pt_sb, 1)
                    act.wait_ge(o_full, hd)
                    act.copy(att[:, bass.DynSlice(hd - 1, 1), :].rearrange("p a b -> p (a b)"),
                             ps[:, 2, 0:S]).then_inc(att_sb, 1)
                    act.copy(orec[:, :, bass.DynSlice((hd - 1) * P, P)],
                             ps[:, 3, 0:S].rearrange("p (t c) -> p t c", t=TT)).then_inc(rec_sb, 1)
                    for t in range(TT):
                        sq = act.activation(junk[:, t, :], ps[:, 3, t * P:(t + 1) * P], ACT.Square,
                                            accum_out=ss[:, bass.DynSlice(hd + (7 + t * HEADS), 1)])
                    sq.then_inc(rec_sb, 1)

            act.wait_ge(gain_g, TT)
            d_body(0, 0, first=True)
            d_body(0, 1)
            with act.Fori(1, HEADS // 2) as i:
                d_body(i, 0)
                d_body(i, 1)
            d_body(HEADS // 2, 0, last=True)
            act.wait_ge(att_sb, HEADS)
            act.wait_ge(tile_done, E0 + HI)
            act.copy(xh[:, 0:HEADS, :], att).then_inc(att_hi, 1)
            for b in range(HEADS // 2):
                act.wait_ge(r_tr, b + 1)
                act.copy(xh[:, HEADS + 2 * b:HEADS + 2 * b + 2, :].rearrange("p a b -> p (a b)"),
                         ps[:, b, :]).then_inc(r_hi, 1)

            with act.Fori(0, (F0 - E0) // RAW) as i:
                for s in range(RAW):
                    hi(i, E0, s)
            act.wait_ge(grp_free, TT * GW)
            norm(1)

            cols(F0, PH, lambda j: qT[:, j, :], ACT.Copy, None)
            cols_end(lambda j: qT[:, j, :], ACT.Copy, 2 * PH - 1, G0)
            for b in range(8):
                act.wait_ge(sc_full, b + 1)
                act.copy(sc[:, 4 * b:4 * b + 4, :].rearrange("p a b -> p (a b)"), ps[:, b, :]).then_inc(sc_sb, 1)

            act.wait_ge(spilled, 16)
            act.wait_ge(sc_full, 8)
            G_AT = ROUTE_TRIPS * TT * PH + 2
            cols(G0, G_AT, lambda j: coef[:, j, :], ACT.Gelu, None)
            act.wait_ge(routed, TT * PH)
            act.activation(best, best, ACT.Exp).then_inc(gexp, 1)
            cols(G0 + RAW * G_AT, NK // 2 - G_AT, lambda j: coef[:, j + 2 * G_AT, :], ACT.Gelu,
                 (lambda i, b: coef[:, 2 * G_AT - 2 + b, :], ACT.Gelu))
            cols_end(lambda j: coef[:, j, :], ACT.Gelu, NK - 1, U0)
            for j in range(3):
                act.wait_ge(it_full, j + 1)
                act.copy(slotT[:, j, :], ps[:, 2 + j, 0:S]).then_inc(it_sb, 1)

            def u_body(i, first):
                for v in range(2):
                    hi(i, U0, 2 * v)
                    act.wait_ge(tile_done, RAW * i + (U0 + 2 * v - 2 * COLT + COLT + HI))
                    if first and v == 0:
                        act.wait_ge(gm_mul, S // 4)
                    act.copy(ch[:, v, :], coef[:, 2 * i + v, :]).then_inc(c_hi, 1)
                    hi(i, U0, 2 * v + 1)

            u_body(0, True)
            with act.Fori(1, NK // 2) as i:
                u_body(i, False)
            act.wait_ge(h_up, 8)
            norm(2)

            def gate_out(i, j):
                act.wait_ge(tile_done, W0 + (2 * i + j + 1) * GRPT + HI)
                for t in range(TT):
                    act.activation(sgate[:, 2 * j + t, :], ps[:, 2 + 2 * j + t, :], ACT.Sigmoid).then_inc(w_sig, 1)

            for i in range(W_GRPS // 2):
                for j in range(2):
                    for s in range(GRPT):
                        hi(4 * i, W0, j * GRPT + s)
                        if s == HI - 1 and (i, j) != (0, 0):
                            gate_out(*((i, 0) if j else (i - 1, 1)))
            gate_out(W_GRPS // 2 - 1, 1)
            for t in range(TT):
                act.wait_ge(w_add, TT * W_GRPS)
                act.activation(hn[:, t, :], h[:, t, :], ACT.Square,
                               accum_out=ss[:, 24 + t:25 + t]).then_inc(f_sq, 1)

        @block.vector
        def _(dve):
            def lo(i, base, s):
                dve.wait_ge(hi_ready, RAW * i + (base + s + 1))
                dve.wait_ge(tile_done, RAW * i + (base + s + 1 - LO + HI))
                dve.tensor_tensor(wlo[:, s % LO, :], raw[:, s % RAW, :], whi[:, s % HI, :].bitcast(F32),
                                  ALU.subtract).then_inc(lo_ready, 1)

            def los(base, tiles):
                with dve.Fori(0, tiles // RAW) as i:
                    for s in range(RAW):
                        lo(i, base, s)

            def norm(k):
                dve.wait_ge(n_rs[k], 1)
                for t in range(TT):
                    dve.tensor_scalar(hn[:, t, :], h[:, t, :], rstd[:, 2 * k + t:2 * k + t + 1], None,
                                      ALU.mult).then_inc(n_row[k], 1)
                for b in range(KC // 2):
                    dve.wait_ge(n_xh[k], b + 1)
                    for c in (2 * b, 2 * b + 1):
                        m = dve.scalar_tensor_tensor(out=xl[:, c, :], in0=ps[:, b, (c % 2) * S:(c % 2 + 1) * S],
                                                     scalar=gain[:, k, c:c + 1], in1=xh[:, c, :].bitcast(F32),
                                                     op0=ALU.mult, op1=ALU.subtract)
                    m.then_inc(n_xl[k], 1)

            class Chain:

                def __init__(self, step):
                    self.step, self.base, self.n = step, 0, 0

                def start(self, base):
                    self.base, self.n = base, 0

                def mark(self, ins):
                    ins.then_inc(self.step, 1)
                    self.n += 1

                def sync(self):
                    dve.wait_ge(self.step, self.base + self.n)

                def link(self, ins):
                    self.mark(ins)
                    self.sync()

            c = Chain(lb_step)
            dve.wait_ge(const_in, 48)
            c.link(dve.tensor_tensor(lb[:, 2, :], lb[:, 0, :], lb[:, 1, :], ALU.max))
            dve.tensor_tensor(lb[:, 3, :], lb[:, 0, :], lb[:, 2, :], ALU.subtract).then_inc(lb_step, 1)
            dve.tensor_tensor(lb[:, 4, :], lb[:, 1, :], lb[:, 2, :], ALU.subtract).then_inc(lb_step, 1)
            c.n += 2
            dve.wait_ge(lb_act, 1)
            c.link(dve.tensor_tensor(lb[:, 7, :], lb[:, 5, :], lb[:, 6, :], ALU.add))
            c.link(dve.reciprocal(lb[:, 2, :], lb[:, 7, :]))
            c.link(dve.tensor_tensor(lb[:, 0, :], lb[:, 5, :], lb[:, 2, :], ALU.mult))
            c.link(dve.tensor_scalar(lb[:, 1, :], lb[:, 0, :], -1.0, 1.0, ALU.mult, ALU.add))
            norm(0)
            los(A0, D0 - A0)

            def halves(v, l):
                return v.rearrange("p (n two h) -> p n two h", two=2, h=HALVES[l])

            pre, soft, mid = Chain(pre_step), Chain(soft_step), Chain(mid_step)
            PRE, SOFT, MID = 2, 2, 2

            def d_body(i, u, first=False, last=False):
                hd = 2 * i + u
                f, fg, logf, b = (fk[:, j, :] for j in range(4))
                if not last:
                    lo(2 * i, D0, 4 * u)
                    pre.start(hd * PRE)
                    if not first:
                        dve.wait_ge(qk_ready, hd)
                    pre.link(dve.tensor_scalar(f, sf[:, hd, :], lb[:, 1, bass.DynSlice(hd, 1)],
                                               lb[:, 0, bass.DynSlice(hd, 1)], ALU.mult, ALU.add))
                    dve.tensor_scalar(kk[:, u, :], f, -1.0, 1.0, ALU.mult, ALU.add)
                    dve.tensor_scalar(fg, f, TINY, None, ALU.max).then_inc(f_ready, 1)
                    lo(2 * i, D0, 4 * u + 1)
                if not first:
                    soft.start((hd - 1) * SOFT)
                    dve.wait_ge(s_full, hd)
                    soft.link(dve.scalar_tensor_tensor(out=pr, in0=ps[:, 2, 0:3 * P], scalar=-SCALE, in1=cmask,
                                                       op0=ALU.mult, op1=ALU.add))
                    dve.tensor_reduce(small[:, 0:1], pr[:, 0:P], AX, ALU.min)
                    dve.tensor_reduce(small[:, 1:2], pr[:, P:3 * P], AX, ALU.min).then_inc(min_ready, 1)
                if not last:
                    dve.wait_ge(logf_ready, hd + 1)
                    pre.link(dve.tensor_tensor_scan(b, ones, logf, 0.0, ALU.mult, ALU.add))
                    for l in range(NL - 1):
                        bl, el = halves(b, l), halves(E[:, l, :], l)
                        mid_ = bl[:, :, 0, HALVES[l] - 1:HALVES[l]].to_broadcast([P, S // 2 // HALVES[l], HALVES[l]])
                        dve.tensor_tensor(el[:, :, 1, :], bl[:, :, 1, :], mid_, ALU.subtract)
                        d = dve.tensor_tensor(el[:, :, 0, :], mid_, bl[:, :, 0, :], ALU.subtract)
                    d.then_inc(d_ready, 1)
                    lo(2 * i, D0, 4 * u + 2)
                if not first:
                    dve.wait_ge(exp_ready, 2 * hd)
                    soft.link(dve.reciprocal(small[:, 4:6], small[:, 2:4]))
                    dve.tensor_scalar(pr[:, 0:P], pr[:, 0:P], small[:, 4:5], None, ALU.mult)
                    dve.tensor_scalar(pr[:, P:3 * P], pr[:, P:3 * P], small[:, 5:6], None,
                                      ALU.mult).then_inc(p_ready, 1)
                    mid.start((hd - 1) * MID)
                    for t, a in ((0, a00), (1, a11)):
                        dve.wait_ge(a_full, 2 * hd - 1 + t)
                        if not (isinstance(hd, int) and hd == 1 and t == 0):
                            dve.wait_ge(a_ready, 2 * hd - 2 + t)
                        mid.link(dve.tensor_tensor(amask.rearrange("p a b -> p (a b)"),
                                                   ps[:, 3 + 2 * t:5 + 2 * t, :].rearrange("p a b -> p (a b)"),
                                                   masks.rearrange("p a b -> p (a b)"), ALU.mult))
                        r = dve.tensor_reduce(a, amask.rearrange("p l t -> p t l"), AX, ALU.add)
                        r.then_inc(a_ready, 1)
                if not last:
                    lo(2 * i, D0, 4 * u + 3)
                    dve.wait_ge(e_ready, hd + 1)
                    qrow = qq[:, bass.DynSlice(hd, 1), :].rearrange("p a b -> p (a b)")
                    for l in range(NL):
                        ql, kl = halves(QL[:, u * NL + l, :], l), halves(KL[:, u * NL + l, :], l)
                        if l < NL - 1:
                            el = halves(E[:, l, :], l)
                            dve.tensor_tensor(ql[:, :, 1, :], halves(qrow, l)[:, :, 1, :], el[:, :, 1, :], ALU.mult)
                            dve.tensor_tensor(kl[:, :, 0, :], halves(kk[:, u, :], l)[:, :, 0, :], el[:, :, 0, :],
                                              ALU.mult)
                        else:
                            dve.tensor_tensor(ql[:, :, 1, :], halves(qrow, l)[:, :, 1, :], halves(f, l)[:, :, 1, :],
                                              ALU.mult)
                            dve.tensor_copy(kl[:, :, 0, :], halves(kk[:, u, :], l)[:, :, 0, :]).then_inc(qk_ready, 1)

            dve.wait_ge(zeroed, 1)
            dve.wait_ge(mask_in, 48)
            d_body(0, 0, first=True)
            d_body(0, 1)
            with dve.Fori(1, HEADS // 2) as i:
                d_body(i, 0)
                d_body(i, 1)
            d_body(HEADS // 2, 0, last=True)
            dve.wait_ge(r_rs, 1)
            for k in range(HEADS):
                for t in range(TT):
                    o = orec[:, t, k * P:(k + 1) * P]
                    m = dve.scalar_tensor_tensor(out=o, in0=o, scalar=rstd[:, 8 + t * HEADS + k:9 + t * HEADS + k],
                                                 in1=gs[:, t, k * P:(k + 1) * P], op0=ALU.mult, op1=ALU.mult)
                m.then_inc(r_row, 1)
            dve.wait_ge(att_hi, 1)
            dve.tensor_tensor(xl[:, 0:HEADS, :], att, xh[:, 0:HEADS, :].bitcast(F32), ALU.subtract).then_inc(att_lo, 1)
            for b in range(HEADS // 2):
                dve.wait_ge(r_hi, b + 1)
                k = slice(HEADS + 2 * b, HEADS + 2 * b + 2)
                dve.tensor_tensor(xl[:, k, :].rearrange("p a b -> p (a b)"), ps[:, b, :],
                                  xh[:, k, :].rearrange("p a b -> p (a b)").bitcast(F32),
                                  ALU.subtract).then_inc(r_lo, 1)

            def h_add(i, j):
                dve.wait_ge(tile_done, i * (2 * GRPT) + (E0 + (j + 1) * GRPT + HI))
                for t in range(TT):
                    dst = h[:, t, bass.DynSlice(i * (2 * GRP) + j * GRP, GRP)]
                    dve.tensor_tensor(dst, ps[:, 2 + 2 * j + t, :], dst, ALU.add).then_inc(grp_free, 1)

            def e_body(i, first):
                for j in range(2):
                    for s in range(GRPT):
                        lo(4 * i, E0, j * GRPT + s)
                        if s == LO - 1 and j:
                            h_add(i, 0)
                        elif s == LO - 1 and not first:
                            h_add(i - 1, 1)

            e_body(0, True)
            with dve.Fori(1, E_GRPS // 2) as i:
                e_body(i, False)
            h_add(E_GRPS // 2 - 1, 1)
            dve.wait_ge(grp_free, TT * GW)
            norm(1)
            los(F0, G0 - F0)

            rt = Chain(rt_step)
            ROUTE = 13

            def hold(k):
                dve.memset(small[:, k:k + 1], 0.0)

            def route(r):
                def split(s):
                    lo(ROUTE_TRIPS * r, G0, s)

                rt.start(r * ROUTE)
                split(0)
                dve.wait_ge(routed, r)
                rt.mark(dve.tensor_scalar(sg, sc[:, bass.DynSlice(2 * r, 2), :], 1.0, None, ALU.mult))
                split(1)
                rt.sync()
                hold(0)
                for k in range(2):
                    m = dve.max(top[:, k, 0:8], sg[:, k, :])
                rt.mark(m)
                split(2)
                rt.sync()
                hold(1)
                for k in range(2):
                    dve.max_index(tixu[:, k, 0:8], top[:, k, 0:8], sg[:, k, :])
                    m = dve.match_replace(sg2[:, k, :], top[:, k, 0:8], sg[:, k, :], NEG)
                rt.mark(m)
                split(3)
                rt.sync()
                hold(2)
                for k in range(2):
                    m = dve.max(top[:, k, 8:TOP], sg2[:, k, :])
                rt.mark(m)
                split(4)
                rt.sync()
                hold(3)
                for k in range(2):
                    dve.max_index(tixu[:, k, 8:TOP], top[:, k, 8:TOP], sg2[:, k, :])
                rt.mark(dve.tensor_tensor(cand, top[:, 0, :].unsqueeze(2).to_broadcast([P, TOP, TOP]),
                                          top[:, 1, :].unsqueeze(1).to_broadcast([P, TOP, TOP]), ALU.add))
                split(5)
                rt.sync()
                cf, cf2 = (v.rearrange("p a b -> p (a b)") for v in (cand, cand2))
                dve.tensor_copy(tix, tixu)
                rt.mark(dve.max(bst[:, 0:8], cf))
                split(6)
                rt.sync()
                hold(4)
                dve.max_index(posu[:, 0:8], bst[:, 0:8], cf)
                rt.mark(dve.match_replace(cf2, bst[:, 0:8], cf, NEG))
                split(7)
                rt.sync()
                hold(5)
                rt.mark(dve.max(bst[:, 8:TOP], cf2))
                split(8)
                rt.sync()
                hold(6)
                rt.mark(dve.max_index(posu[:, 8:TOP], bst[:, 8:TOP], cf2))
                split(9)
                rt.sync()
                dve.tensor_scalar(best[:, r, :], bst, bst[:, 0:1], None, ALU.subtract)
                dve.tensor_scalar(abu[:, 0, :], posu, 4, None, ALU.logical_shift_right)
                rt.mark(dve.tensor_scalar(abu[:, 1, :], posu, TOP - 1, None, ALU.bitwise_and))
                split(10)
                rt.sync()
                rt.mark(dve.tensor_copy(ab, abu))
                split(11)
                rt.sync()
                ohf = oh.rearrange("p a b c -> p (a b) c")
                rt.mark(dve.tensor_tensor(ohf, ab.rearrange("p a b -> p (a b)").unsqueeze(2).to_broadcast([P, 2 * TOP, TOP]),
                                          iota[:, 0:TOP].unsqueeze(1).to_broadcast([P, 2 * TOP, TOP]), ALU.is_equal))
                rt.sync()
                for k in range(2):
                    m = dve.tensor_tensor(oh[:, k, :, :], oh[:, k, :, :],
                                          tix[:, k, :].unsqueeze(1).to_broadcast([P, TOP, TOP]), ALU.mult)
                rt.mark(m)
                rt.sync()
                assert rt.n == ROUTE
                dve.tensor_reduce(i1[:, r, :], oh[:, 0, :, :], AX, ALU.add)
                dve.tensor_reduce(i2[:, r, :], oh[:, 1, :, :], AX, ALU.add).then_inc(routed, 1)

            dve.wait_ge(sc_sb, 8)
            with dve.Fori(0, TT * PH) as r:
                route(r)
            los(G0 + TT * PH * RAW * ROUTE_TRIPS, U0 - G0 - TT * PH * RAW * ROUTE_TRIPS)
            gc = Chain(g_step)
            dve.wait_ge(gexp, 1)
            gc.link(dve.tensor_reduce(gsum, best, AX, ALU.add))
            gc.link(dve.reciprocal(gsum, gsum))
            dve.tensor_tensor(gate, best, gsum.unsqueeze(2).to_broadcast([P, TT * PH, TOP]), ALU.mult).then_inc(gates, 1)

            def onehots(i, u):
                b = 2 * i + u
                dve.tensor_tensor(oneL[:, 4 * u:4 * u + 4, :],
                                  slotT[:, 0, bass.DynSlice(4 * b, 4)].unsqueeze(2).to_broadcast([P, 4, P]),
                                  iota.unsqueeze(1).to_broadcast([P, 4, P]), ALU.is_equal)
                for t in range(4):
                    m = dve.tensor_scalar(gateR[:, 4 * u + t, :], iota, slotT[:, 1, bass.DynSlice(4 * b + t, 1)],
                                          slotT[:, 2, bass.DynSlice(4 * b + t, 1)], ALU.is_equal, ALU.mult)
                m.then_inc(oh_ready, 1)

            def apply(b, u):
                dve.wait_ge(gm_full, b + 1)
                dst = coef_t[:, bass.DynSlice(4 * b, 4), :]
                dve.tensor_tensor(dst, dst, ps[:, 5 + u, :].rearrange("p (t e) -> p t e", t=4),
                                  ALU.mult).then_inc(gm_mul, 1)

            dve.wait_ge(it_sb, 3)
            onehots(0, 0)
            onehots(0, 1)
            apply(0, 0)
            with dve.Fori(1, S // 8) as i:
                onehots(i, 0)
                apply(2 * i - 1, 1)
                onehots(i, 1)
                apply(2 * i, 0)
            apply(S // 4 - 1, 1)

            def u_body(i):
                for v in range(2):
                    lo(i, U0, 2 * v)
                    dve.wait_ge(c_hi, 2 * i + (v + 1))
                    dve.tensor_tensor(cl[:, v, :], coef[:, 2 * i + v, :], ch[:, v, :].bitcast(F32),
                                      ALU.subtract).then_inc(c_lo, 1)
                    lo(i, U0, 2 * v + 1)

            with dve.Fori(0, NK // 2) as i:
                u_body(i)
            dve.wait_ge(h_back, 16)
            dve.wait_ge(tile_done, W0 + HI)
            for t in range(TT):
                for g in range(4):
                    dst = h[:, t, g * GRP:(g + 1) * GRP]
                    dve.tensor_tensor(dst, ps[:, 4 * t + g, :], dst, ALU.add).then_inc(h_up, 1)
            dve.wait_ge(h_up, 8)
            norm(2)

            def w_out(i, j):
                for t in range(TT):
                    n = TT * (2 * i + j) + t
                    dve.wait_ge(w_sig, n + 1)
                    if n >= 2 * TT:
                        dve.wait_ge(w_add, n - 2 * TT + 1)
                    dve.tensor_tensor(ple_m[:, 2 * j + t, :], ps[:, 6 * j + t, :], sgate[:, 2 * j + t, :],
                                      ALU.mult).then_inc(grp_free, 1)
                    dve.wait_ge(grp_free, TT * GW + n + 1)
                    dst = h[:, t, (2 * i + j) * GRP:(2 * i + j + 1) * GRP]
                    dve.tensor_tensor(dst, ple_m[:, 2 * j + t, :], dst, ALU.add).then_inc(w_add, 1)

            for i in range(W_GRPS // 2):
                for j in range(2):
                    for s in range(GRPT):
                        lo(4 * i, W0, j * GRPT + s)
                        if s == HI - 1 and (i, j) != (0, 0):
                            w_out(*((i, 0) if j else (i - 1, 1)))
            w_out(W_GRPS // 2 - 1, 1)
            dve.wait_ge(f_rs, 1)
            dve.wait_ge(ple_in, 48)
            for t in range(TT):
                dve.scalar_tensor_tensor(out=orow[:, t, :], in0=h[:, t, :], scalar=rstd[:, 24 + t:25 + t],
                                         in1=gf_row, op0=ALU.mult, op1=ALU.mult).then_inc(f_row, 1)

        @block.tensor
        def _(pe):
            def norm(k):
                pe.wait_ge(n_row[k], TT)
                if k == 0:
                    pe.wait_ge(const_in, 48)
                for c in range(KC):
                    for t in range(TT):
                        mm = pe.transpose(ps[:, c // 2, (c % 2) * S + t * P:(c % 2) * S + (t + 1) * P],
                                          hn[:, t, c * P:(c + 1) * P], ident)
                    if c % 2:
                        mm.then_inc(n_tr[k], 1)
                    if k == 0 and c == 0:
                        pe.sem_inc(tile_done, HI)
                pe.wait_ge(n_xl[k], KC // 2)

            def parts(s, width):
                return (w.rearrange("p (k c) -> p k c", c=width) for w in (whi[:, s % HI, :], wlo[:, s % LO, :]))

            def col_tile(i, base, s, bank, second, free=None):
                if free is not None:
                    pe.wait_ge(col_free, free)
                pe.wait_ge(lo_ready, RAW * i + (base + s + 1))
                wh, wl = parts(s, P)
                for k in range(KPC):
                    kc = second * KPC + k
                    pe.matmul(col_ps(bank), wh[:, k, :], xh[:, kc, :], start=(kc == 0), stop=False)
                    pe.matmul(col_ps(bank), wh[:, k, :], xl[:, kc, :], start=False, stop=False)
                    mm = pe.matmul(col_ps(bank), wl[:, k, :], xh[:, kc, :], start=False, stop=(kc == KC - 1))
                mm.then_inc(tile_done, 1)

            def cols(base, c0, trips, first=False):
                def body(i, free):
                    for s in range(RAW):
                        col_tile(i, base, s, s // COLT, s % COLT,
                                 2 * i + (c0 + s // COLT - 1) if free and s % COLT == 0 else None)

                if first:
                    body(0, False)
                with pe.Fori(1 if first else 0, trips) as i:
                    body(i, True)

            def grp_tile(i, base, s, kt, bank):
                pe.wait_ge(lo_ready, RAW * i + (base + s + 1))
                wh, wl = parts(s, GRP)
                for t in range(TT):
                    tk = slice(t * P, (t + 1) * P)
                    for k in range(KPG):
                        kc = kt * KPG + k
                        o = ps[:, bank + t, :]
                        pe.matmul(o, xh[:, kc, tk], wh[:, k, :], start=(kc == 0), stop=False)
                        pe.matmul(o, xl[:, kc, tk], wh[:, k, :], start=False, stop=False)
                        mm = pe.matmul(o, xh[:, kc, tk], wl[:, k, :], start=False, stop=(kc == KC - 1))
                mm.then_inc(tile_done, 1)

            def groups(base, g0, pairs, first=False, extra=None):
                def body(i, free):
                    for j in range(2):
                        if free:
                            pe.wait_ge(grp_free, TT * 2 * i + TT * (g0 + j - 1))
                        if extra is not None:
                            extra(i, j)
                        for s in range(GRPT):
                            grp_tile(4 * i, base, j * GRPT + s, s, 2 + 2 * j)

                if first:
                    body(0, False)
                with pe.Fori(1 if first else 0, pairs) as i:
                    body(i, True)

            norm(0)
            cols(A0, CA, A_COLS // 2, first=True)
            groups(B0, GB, B_GRPS // 2, first=True)

            def d_body(i, u, first=False, last=False):
                hd = 2 * i + u
                v = 1 - u
                if not last:
                    col_tile(2 * i, D0, 4 * u, 0, 0, 2 * hd + (CD - 1))
                if not first:
                    pe.wait_ge(col_free, 2 * hd + CD)
                    if isinstance(hd, int) and hd == 1:
                        pe.wait_ge(grp_free, TT * B_GRPS)
                    else:
                        pe.wait_ge(att_sb, hd - 1)
                    q, k = qk[:, 2 * v, :], qk[:, 2 * v + 1, :]
                    pe.matmul(ps[:, 2, 0:P], q[:, 0:P], k[:, 0:P], start=True, stop=True)
                    pe.matmul(ps[:, 2, P:3 * P], q[:, P:S], k, start=True, stop=True).then_inc(s_full, 1)
                if not last:
                    col_tile(2 * i, D0, 4 * u + 1, 0, 1)
                if not first:
                    pe.wait_ge(qk_ready, hd)
                    if not (isinstance(hd, int) and hd == 1):
                        pe.wait_ge(rec_sb, 2 * hd - 2)
                    for t in range(TT):
                        tk = slice(t * P, (t + 1) * P)
                        if t == 0:
                            pe.matmul(ps[:, 7, 3 * P:4 * P], KL[:, v * NL, 0:P], QL[:, v * NL, P:S],
                                      start=True, stop=True)
                        for l in range(1, NL + 1):
                            o = ps[:, 3 + 2 * t + (l - 1) // 4, (l - 1) % 4 * P:((l - 1) % 4 + 1) * P]
                            if l < NL:
                                pe.matmul(o, KL[:, v * NL + l, tk], QL[:, v * NL + l, tk], start=True, stop=True)
                            else:
                                qd = qq[:, bass.DynSlice(hd - 1, 1), tk].rearrange("p a b -> p (a b)")
                                mm = pe.matmul(o, kk[:, v, tk], qd, start=True, stop=True)
                        mm.then_inc(a_full, 1)
                if not last:
                    col_tile(2 * i, D0, 4 * u + 2, 1, 0, 2 * hd + CD)
                if not first:
                    pe.wait_ge(ax_ready, hd)
                    pe.wait_ge(p_ready, hd)
                    for j in range(3):
                        mm = pe.transpose(ps[:, 7, j * P:(j + 1) * P], pr[:, j * P:(j + 1) * P], ident)
                    mm.then_inc(pt_full, 1)
                if not last:
                    col_tile(2 * i, D0, 4 * u + 3, 1, 1)
                if not first:
                    pe.wait_ge(pt_sb, hd)
                    pe.wait_ge(v_ready, hd)
                    pe.matmul(ps[:, 2, 0:P], vh[:, 0, :], pT[:, 0:P], start=True, stop=True)
                    pe.matmul(ps[:, 2, P:S], vh[:, 0, :], pT[:, P:S], start=True, stop=False)
                    pe.matmul(ps[:, 2, P:S], vh[:, 1, :], pT[:, S:3 * P], start=False, stop=True)
                    pe.wait_ge(a_ready, 2 * hd)
                    vr = [gi[:, t, bass.DynSlice((hd - 1) * P, P)] for t in range(TT)]
                    pe.matmul(ps[:, 3, 0:P], a00, vr[0], start=True, stop=True)
                    pe.matmul(ps[:, 3, P:S], a01, vr[0], start=True, stop=False)
                    pe.matmul(ps[:, 3, P:S], a11, vr[1], start=False, stop=True).then_inc(o_full, 1)

            d_body(0, 0, first=True)
            d_body(0, 1)
            with pe.Fori(1, HEADS // 2) as i:
                d_body(i, 0)
                d_body(i, 1)
            d_body(HEADS // 2, 0, last=True)
            pe.wait_ge(att_sb, HEADS)
            for c in range(HEADS):
                pe.wait_ge(r_row, c + 1)
                for t in range(TT):
                    mm = pe.transpose(ps[:, c // 2, (c % 2) * S + t * P:(c % 2) * S + (t + 1) * P],
                                      orec[:, t, c * P:(c + 1) * P], ident)
                if c % 2:
                    mm.then_inc(r_tr, 1)
            pe.wait_ge(att_lo, 1)
            pe.wait_ge(r_lo, HEADS // 2)

            groups(E0, GE, E_GRPS // 2)
            norm(1)
            cols(F0, CF, PH)
            pe.wait_ge(sk_in, 16)
            pe.wait_ge(col_free, CG)
            for t in range(TT):
                for g in range(2 * PH):
                    n = t * 2 * PH + g
                    mm = pe.matmul(ps[:, n // 4, n % 4 * P:(n % 4 + 1) * P], qT[:, g, t * P:(t + 1) * P],
                                   sk[:, g, :], start=True, stop=True)
                    if n % 4 == 3:
                        mm.then_inc(sc_full, 1)
            pe.wait_ge(sc_sb, 2)
            cols(G0, CG, NK // 2)

            pe.wait_ge(gates, 1)
            pe.wait_ge(sc_sb, 8)
            for j, v in enumerate((i1, i2, gate)):
                flat = v.rearrange("p a b -> p (a b)")
                for t in range(TT):
                    mm = pe.transpose(ps[:, 2 + j, t * P:(t + 1) * P], flat[:, t * P:(t + 1) * P], ident)
                mm.then_inc(it_full, 1)

            def gate_products(i, first):
                for u in range(2):
                    pe.wait_ge(oh_ready, 2 * i + (u + 1))
                    if not first:
                        pe.wait_ge(gm_mul, 2 * i + (u - 1))
                    for t in range(4):
                        mm = pe.matmul(ps[:, 5 + u, t * P:(t + 1) * P], oneL[:, 4 * u + t, :].bitcast(F32),
                                       gateR[:, 4 * u + t, :], start=True, stop=True)
                    mm.then_inc(gm_full, 1)

            gate_products(0, True)
            with pe.Fori(1, S // 8) as i:
                gate_products(i, False)

            def u_body(i, first=False, last=False):
                for s in range(RAW):
                    v, dh = s // 2, s % 2
                    if dh == 0:
                        pe.wait_ge(c_lo, 2 * i + (v + 1))
                    pe.wait_ge(lo_ready, RAW * i + (U0 + s + 1))
                    wh, wl = parts(s, GRP)
                    st, sp_ = first and v == 0, last and v == 1
                    for t in range(TT):
                        tk = slice(t * P, (t + 1) * P)
                        for k in range(2):
                            o = ps[:, 4 * t + 2 * dh + k, :]
                            pe.matmul(o, ch[:, v, tk], wh[:, k, :], start=st, stop=False)
                            pe.matmul(o, cl[:, v, tk], wh[:, k, :], start=False, stop=False)
                            mm = pe.matmul(o, ch[:, v, tk], wl[:, k, :], start=False, stop=sp_)
                    mm.then_inc(tile_done, 1)

            u_body(0, first=True)
            with pe.Fori(1, NK // 2 - 1) as i:
                u_body(i)
            u_body(NK // 2 - 1, last=True)
            norm(2)

            def embed(i, j):
                for t in range(TT):
                    for k in range(PK):
                        pe.matmul(ps[:, 6 * j + t, :], ple_p[:, k, t * P:(t + 1) * P],
                                  ple_w[:, k, bass.DynSlice(i * (2 * GRP) + j * GRP, GRP)],
                                  start=(k == 0), stop=(k == PK - 1))

            pe.wait_ge(ple_in, 48)
            groups(W0, GW, W_GRPS // 2, extra=embed)


_OUT = ((1, S, D), "float32")


def blocks_of_columns(w):
    n = w.shape[1] // P
    return w.reshape(COLT, KPC, P, n, P).transpose(3, 0, 2, 1, 4).reshape(n * COLT, P, TILE)


def groups_of_columns(w):
    n = w.shape[1] // GRP
    return w.reshape(GRPT, KPG, P, n, GRP).transpose(3, 0, 2, 1, 4).reshape(n * GRPT, P, TILE)


def kernel(x, p, norm_mix, w_in, lb_logits, hgrn_norm, w_out, norm_ffn, peer_query, peer_sub_keys, peer_down,
           peer_up, norm_ple, w_ple, w_ple_gate, norm_final):
    import concourse.bacc as bacc
    from concourse.bass_utils import run_bass_kernel_spmd

    x, p, w_in, w_out, wq, wg = (np.asarray(a) for a in (x, p, w_in, w_out, peer_query, w_ple_gate))
    aq, ak, av, gq, gf, gi, gg = (w_in[0][:, k * HW:(k + 1) * HW] for k in range(7))
    heads = [a[:, k * P:(k + 1) * P] for k in range(HEADS) for a in (aq, ak)]
    rows = np.arange(P)
    s, t = rows[:, None], rows[None, :]
    level = [(s // (2 * m) == t // (2 * m)) & (s % (2 * m) < m) & (t % (2 * m) >= m) for m in HALVES[1:]]
    level_masks = np.stack(level + [s == t], 1).reshape(P, NL * P).astype(np.float32)
    hide = np.where(t > s, np.float32(-NEG), np.float32(0))
    consts = np.concatenate([np.eye(P), np.tile(rows, (P, 1))], 1).astype(np.float32)
    mix_consts = np.concatenate([hide, np.zeros((P, P)), hide, np.ones((P, S))], 1).astype(np.float32)
    gains = np.stack([np.asarray(g).reshape(KC, P).T for g in (norm_mix, norm_ffn, norm_ple)], 1)
    arrays = {
        "x": x.reshape(S, D),
        "win_t": blocks_of_columns(np.concatenate([gf, gq] + heads, 1)),
        "win_n": groups_of_columns(np.concatenate([gi, gg, av], 1)),
        "wout": groups_of_columns(w_out[0]),
        "wq": blocks_of_columns(wq[0]),
        "down": np.asarray(peer_down).reshape(NK, NK, COLT, KPC, P).transpose(1, 2, 4, 3, 0).reshape(-1, P, TILE),
        "up": np.asarray(peer_up).reshape(NK, NK, D),
        "wgate": groups_of_columns(wg[0]),
        "gains": gains,
        "lbl": np.asarray(lb_logits).reshape(2, HEADS, P).transpose(2, 0, 1),
        "gain_h": np.asarray(hgrn_norm).reshape(HW),
        "gain_f": np.asarray(norm_final).reshape(D),
        "skt": np.asarray(peer_sub_keys).reshape(2 * PH, NK, P).transpose(2, 0, 1).reshape(P, 2 * PH * NK),
        "pt": p.reshape(S, PK, P).transpose(2, 1, 0).reshape(P, PK * S),
        "wple": np.asarray(w_ple).reshape(PK, P, D).transpose(1, 0, 2).reshape(P, PK * D),
        "consts": consts,
        "mix_consts": mix_consts,
        "level_masks": level_masks,
    }
    arrays = {f"in_{k}": np.ascontiguousarray(v) for k, v in arrays.items()}
    nc = bacc.Bacc("TRN2", target_bir_lowering=False, num_devices=1, dynamic_dma_scratch_size=1024)
    ins = {k: nc.dram_tensor(k, a.shape, mybir.dt.from_np(a.dtype), kind="ExternalInput").ap()
           for k, a in arrays.items()}
    o = nc.dram_tensor("out_0", [S, D], F32, kind="ExternalOutput").ap()
    ins["in_up"] = ins["in_up"].rearrange("a b d -> b a d")
    program(nc, out=o, **{k[3:]: v for k, v in ins.items()})
    r = run_bass_kernel_spmd(nc, [arrays], core_ids=[0])
    return r.results[0]["out_0"].reshape(_OUT[0])
```

```python
from contextlib import ExitStack

import numpy as np

import concourse.bass as bass
from concourse import mybir

F32 = mybir.dt.float32
F32R = mybir.dt.float32r
U32 = mybir.dt.uint32
ALU = mybir.AluOpType
ACT = mybir.ActivationFunctionType
AX = mybir.AxisListType.X

P = 128
D = 2048
S = 256
TT = S // P
KC = D // P
HEADS = 8
HW = HEADS * P
GRP = 512
TILE = 1024
RAW = 4
HI = 4
LO = 2
COLT = KC * P // TILE
GRPT = KC * GRP // TILE
KPC = TILE // P
KPG = TILE // GRP
HALVES = [128, 64, 32, 16, 8, 4, 2, 1]
NL = len(HALVES)
PH = 8
NK = 128
TOP = 16
ROUTE_TILES = 8
DIRECT = TT * PH * ROUTE_TILES // COLT
GATED = 4
GT0 = DIRECT // 2
GTRIPS = NK // 2 - GT0 - 2
TAIL = S // GATED - 2 * GTRIPS
PLE = 256
PK = PLE // P
EPS = 1e-6
SCALE = float(P) ** -0.5
NEG = -3.0e38
MISC = 2944
TINY = 2.0 ** -64

A_COLS, B_GRPS, D_COLS, E_GRPS, F_COLS, W_GRPS = 16, 6, 16, D // GRP, 2 * PH, D // GRP
A0 = 0
B0 = A0 + A_COLS * COLT
D0 = B0 + B_GRPS * GRPT
E0 = D0 + D_COLS * COLT
F0 = E0 + E_GRPS * GRPT
G0 = F0 + F_COLS * COLT
U0 = G0 + NK * COLT
W0 = U0 + NK * D // TILE
CA, CD, CF, CG = 0, A_COLS, A_COLS + D_COLS, A_COLS + D_COLS + F_COLS
R_BANKS = [0, 1, 6, 7]
GB, GE, GW = 0, B_GRPS, B_GRPS + E_GRPS


def program(nc, x, win_t, win_n, wout, wq, down, up, wgate, gains, lbl, gain_h, gain_f, skt, pt, wple,
            consts, mix_consts, level_masks, out):
    with ExitStack() as ctx:
        def sb(name, shape, dt=F32):
            return ctx.enter_context(nc.sbuf_tensor(name, shape, dt))

        def sem(name):
            return ctx.enter_context(nc.semaphore(name))

        h_spill = nc.dram_tensor("h_spill", [P, TT * D], F32, kind="Internal").ap()
        g_spill = nc.dram_tensor("g_spill", [NK - DIRECT, P, S], F32, kind="Internal").ap()

        arena = sb("arena", [P, NK * S])
        raw = sb("raw", [P, RAW, TILE])
        whi = sb("whi", [P, HI, TILE], F32R)
        wlo = sb("wlo", [P, LO, TILE], F32R)
        xh = sb("xh", [P, KC, S], F32R)
        xl = sb("xl", [P, KC, S], F32R)
        cst = sb("cst", [P, 2 * P])
        gain = sb("gain", [P, 3, KC])
        ss = sb("ss", [P, 32])
        rstd = sb("rstd", [P, 32])
        half = sb("half", [P, 16])
        lb = sb("lb", [P, 8, HEADS])
        small = sb("small", [P, 8])
        ch = sb("ch", [P, 2, S], F32R)
        cl = sb("cl", [P, 2, S], F32R)
        misc = sb("misc", [P, MISC])
        stage = sb("stage", [P, 2, S])

        def view(of, base, shape):
            v = of[:, base:base + int(np.prod(shape))]
            names = "abc"[:len(shape)]
            return v if len(shape) == 1 else v.rearrange(
                f"p ({' '.join(names)}) -> p {' '.join(names)}", **dict(zip(names, shape)))

        ident, iota = cst[:, 0:P], cst[:, P:2 * P]

        at = {"arena": 0, "misc": 0}

        def take(*shape, of="arena"):
            v = view(arena if of == "arena" else misc, at[of], shape)
            at[of] += int(np.prod(shape))
            return v

        h = take(TT, D)
        hn = view(arena, at["arena"], (TT, D))
        fg = take(HEADS, S)
        qq = take(HEADS, S)
        take(B_GRPS // 2, TT, HW)
        tok = arena[:, at["arena"] - B_GRPS // 2 * TT * HW:at["arena"]]

        def tokens(which):
            return tok[:, which * TT * HW:(which + 1) * TT * HW].rearrange("p (t c) -> p t c", t=TT)

        gi, gs, va = tokens(0), tokens(1), tokens(2)
        orec = take(TT, HW)
        grow = orec[:, 0, :]
        QL_AT = at["arena"]
        QL, KL = take(2 * NL, S), take(2 * NL, S)
        E = take(NL - 1, S)
        masks = take(NL, P)
        amask = take(NL, P)
        a00, a01, a11 = take(P), take(P), take(P)
        mix_c = take(3 * P + S)
        cmask, ones = mix_c[:, 0:3 * P], mix_c[:, 3 * P:]
        qk = take(4, S)
        att = take(HEADS, S)
        bsum = att
        assert at["arena"] <= NK * S
        kk = take(2, S, of="misc")
        pr = take(3 * P, of="misc")
        pT = take(3 * P, of="misc")
        vh = take(2, P, of="misc")
        junk = take(2, P, of="misc")
        assert at["misc"] <= MISC
        sk = view(arena, 8192, (2 * PH, NK))
        qT = view(arena, 10240, (2 * PH, S))
        SC_AT = NK * S - TT * 2 * PH * NK
        sc = view(arena, SC_AT, (TT * 2 * PH, NK))
        at["misc"] = 0
        i1, i2, best, gate = (take(TT * PH, TOP, of="misc") for _ in range(4))
        R = at["misc"]
        sg, sg2 = take(2, NK, of="misc"), take(2, NK, of="misc")
        top, tixu, tix = take(2, TOP, of="misc"), take(2, TOP, of="misc").bitcast(U32), take(2, TOP, of="misc")
        cand, cand2 = take(TOP, TOP, of="misc"), take(TOP, TOP, of="misc")
        bst, posu = take(TOP, of="misc"), take(TOP, of="misc").bitcast(U32)
        abu, ab = take(2, TOP, of="misc").bitcast(U32), take(2, TOP, of="misc")
        oh = take(2, TOP, TOP, of="misc")
        isel = take(2, TOP, of="misc")
        gsum = take(TT * PH, of="misc")
        assert at["misc"] <= MISC
        at["misc"] = R
        slotT = take(3, S, of="misc")
        gateR = take(2 * GATED, P, of="misc")
        oneL = view(misc, 0, (2 * GATED, P))
        assert at["misc"] <= MISC and 2 * GATED * P <= R
        coef = view(arena, 0, (NK, S))
        coef_t = arena[:, :].rearrange("p (e t) -> p t e", t=S)
        ple_w = view(arena, 8192, (PK, D))
        ple_p = view(arena, 12288, (PK, S))
        gf_row = view(arena, 12800, (D,))
        sgate = view(arena, 16384, (2 * TT, GRP))
        ple_m = view(arena, 18432, (2 * TT, GRP))
        orow = view(arena, 20480, (TT, D))

        ps = ctx.enter_context(nc.psum_tensor("ps", [P, 8, 512], F32))

        def col_ps(bank):
            return ps[:, bank, 0:S]

        const_in = sem("const_in")
        mask_in = sem("mask_in")
        h_in = [sem(f"h_in{t}") for t in range(TT)]
        raw_in = [sem(f"raw_in{i}") for i in range(RAW)]
        hi_ready, lo_ready, tile_done = sem("hi_ready"), sem("lo_ready"), sem("tile_done")
        col_free = sem("col_free")
        grp_free = sem("grp_free")
        lb_step, lb_act = sem("lb_step"), sem("lb_act")
        NORMS = ["mix", "ffn", "ple"]
        n_sq, n_rs, n_row, n_tr, n_xh, n_xl = (
            [sem(f"n_{what}_{n}") for n in NORMS] for what in ("sq", "rs", "row", "tr", "xh", "xl"))
        pool_step, zeroed = sem("pool_step"), sem("zeroed")
        gain_g = sem("gain_g")
        f_step, f_ready, logf_ready, b_ready = (sem(n) for n in ("f_step", "f_ready", "logf_ready", "b_ready"))
        kk_ready, d_ready, e_ready, qk_ready = (sem(n) for n in ("kk_ready", "d_ready", "e_ready", "qk_ready"))
        soft_step, mid_step = sem("soft_step"), sem("mid_step")
        s_full, min_ready, exp_ready, p_ready = (sem(n) for n in ("s_full", "min_ready", "exp_ready", "p_ready"))
        a_full, a_ready, ax_ready = sem("a_full"), sem("a_ready"), sem("ax_ready")
        pt_full, pt_sb, v_ready = sem("pt_full"), sem("pt_sb"), sem("v_ready")
        o_full, att_sb, rec_sb = sem("o_full"), sem("att_sb"), sem("rec_sb")
        att_hi, att_lo = sem("att_hi"), sem("att_lo")
        r_rs, r_row, r_tr, r_hi, r_lo = (sem(f"r_{n}") for n in ("rs", "row", "tr", "hi", "lo"))
        spilled, sk_in, sc_full, sc_sb = sem("spilled"), sem("sk_in"), sem("sc_full"), sem("sc_sb")
        rt_step, routed, gexp, g_step, gates = (sem(n) for n in ("rt_step", "routed", "gexp", "g_step", "gates"))
        it_full, it_sb = sem("it_full"), sem("it_sb")
        oh_ready, gm_full, gm_mul = sem("oh_ready"), sem("gm_full"), sem("gm_mul")
        g_pre = sem("g_pre")
        g_out = [sem(f"g_out{b}") for b in range(2)]
        st_in = [sem(f"st_in{b}") for b in range(2)]
        c_mul, c_hi, c_lo = sem("c_mul"), sem("c_hi"), sem("c_lo")
        h_back, h_up, ple_in = sem("h_back"), sem("h_up"), sem("ple_in")
        w_sig, w_add = sem("w_sig"), sem("w_add")
        f_sq, f_rs, f_row, stored = sem("f_sq"), sem("f_rs"), sem("f_row"), sem("stored")

        def halves(v, l):
            return v.rearrange("p (n two h) -> p n two h", two=2, h=HALVES[l])

        block = ctx.enter_context(nc.Block())

        @block.sync
        def _(sp):
            for t in range(TT):
                sp.dma_start(h[:, t, :], x[t * P:(t + 1) * P, :]).then_inc(h_in[t], 16)
            sp.dma_start(cst[:], consts).then_inc(const_in, 16)
            sp.dma_start(gain[:], gains).then_inc(const_in, 16)
            sp.dma_start(lb[:, 0:2, :], lbl).then_inc(const_in, 16)

            def load(src, s, split):
                if split is not None:
                    sp.wait_ge(lo_ready, split)
                sp.dma_start(raw[:, s, :], src).then_inc(raw_in[s], 16)

            def stream(src, base, tiles, first=0):
                with sp.Fori(0, tiles // RAW) as i:
                    for s in range(RAW):
                        load(src[RAW * i + (first + s)], s, RAW * i + (base + s - RAW + 1))

            for s in range(RAW):
                load(win_t[s], s, None)
            sp.dma_start(masks.rearrange("p a b -> p (a b)"), level_masks).then_inc(mask_in, 16)
            sp.dma_start(grow, gain_h.partition_broadcast(P)).then_inc(mask_in, 16)
            sp.dma_start(mix_c, mix_consts).then_inc(mask_in, 16)
            with sp.Fori(1, A_COLS * COLT // RAW) as i:
                for s in range(RAW):
                    load(win_t[RAW * i + s], s, RAW * i + (s - RAW + 1))
            stream(win_n, B0, D0 - B0)
            stream(win_t, D0, E0 - D0, A_COLS * COLT)
            stream(wout, E0, F0 - E0)
            sp.wait_ge(grp_free, TT * GW)
            sp.dma_start(sk.rearrange("p a b -> p (a b)"), skt).then_inc(sk_in, 16)
            sp.dma_start(h_spill, h.rearrange("p a b -> p (a b)")).then_inc(spilled, 16)
            stream(wq, F0, G0 - F0)
            stream(down, G0, U0 - G0)
            def up_tiles(i, back=False, first=False):
                for s in range(RAW):
                    if back and s % COLT == 0:
                        v = s // COLT
                        if not first:
                            sp.wait_ge(c_mul, 2 * i + (v - DIRECT - 1))
                        sp.dma_start(stage[:, v, :], g_spill[2 * i + (v - DIRECT)]).then_inc(st_in[v], 16)
                    load(up[2 * i + s // 2, :, (s % 2) * TILE:(s % 2 + 1) * TILE], s,
                         RAW * i + (U0 + s - RAW + 1))

            with sp.Fori(0, GT0) as i:
                up_tiles(i)
            for b in range(2):
                sp.wait_ge(g_out[b], 16 * (NK - DIRECT) // 2)
            up_tiles(GT0, back=True, first=True)
            with sp.Fori(GT0 + 1, NK // 2) as i:
                up_tiles(i, back=True)
            sp.wait_ge(c_lo, NK)
            sp.dma_start(h.rearrange("p a b -> p (a b)"), h_spill).then_inc(h_back, 16)
            sp.dma_start(ple_w.rearrange("p a b -> p (a b)"), wple).then_inc(ple_in, 16)
            sp.dma_start(ple_p.rearrange("p a b -> p (a b)"), pt).then_inc(ple_in, 16)
            sp.dma_start(gf_row, gain_f.partition_broadcast(P)).then_inc(ple_in, 16)
            stream(wgate, W0, W_GRPS * GRPT)
            for t in range(TT):
                sp.wait_ge(f_row, t + 1)
                sp.dma_start(out[t * P:(t + 1) * P, :], orow[:, t, :]).then_inc(stored, 16)
            sp.wait_ge(stored, 16 * TT)

        @block.gpsimd
        def _(pool):
            steps = 0

            def power(first, width, count, ready, need, done):
                nonlocal steps
                v = ss[:, first:first + width]
                pool.wait_ge(ready, need)
                pool.tensor_scalar(v, v, 1.0 / count, EPS, ALU.mult, ALU.add).then_inc(pool_step, 1)
                steps += 1
                pool.wait_ge(pool_step, steps)
                pool.tensor_tensor(rstd[:, first:first + width], v, half[:, 0:width], ALU.pow).then_inc(done, 1)

            steps += 1
            pool.memset(half[:], -0.5).then_inc(pool_step, 1)
            pool.memset(arena[:, QL_AT:QL_AT + 4 * NL * S], 0.0).then_inc(zeroed, 1)
            power(0, TT, D, n_sq[0], TT, n_rs[0])
            pool.wait_ge(grp_free, TT * 4)
            pool.wait_ge(mask_in, 48)
            for t in range(TT):
                pool.tensor_tensor(gs[:, t, :], gs[:, t, :], grow, ALU.mult).then_inc(gain_g, 1)
            def pre(i, u, first=False):
                if not first:
                    pool.wait_ge(qk_ready, i)
                b = bsum[:, bass.DynSlice(i, 1), :].rearrange("p a b -> p (a b)")
                for l in range(NL - 1):
                    bl, el = halves(b, l), halves(E[:, l, :], l)
                    mid = bl[:, :, 0, HALVES[l] - 1:HALVES[l]].to_broadcast([P, S // 2 // HALVES[l], HALVES[l]])
                    pool.tensor_tensor(el[:, :, 1, :], bl[:, :, 1, :], mid, ALU.subtract)
                    d = pool.tensor_tensor(el[:, :, 0, :], mid, bl[:, :, 0, :], ALU.subtract)
                d.then_inc(d_ready, 1)
                if not (isinstance(i, int) and i < 2):
                    pool.wait_ge(a_full, 2 * i - 2)
                pool.tensor_tensor(kk[:, u, :], ones, fg[:, bass.DynSlice(i, 1), :].rearrange("p a b -> p (a b)"),
                                   ALU.subtract).then_inc(kk_ready, 1)

            def v_copy(i, first=False):
                if not first:
                    pool.wait_ge(o_full, i)
                pool.tensor_copy(vh, va[:, :, bass.DynSlice(i * P, P)]).then_inc(v_ready, 1)

            pool.wait_ge(b_ready, 1)
            pre(0, 0, True)
            pre(1, 1)
            pool.wait_ge(grp_free, TT * B_GRPS)
            v_copy(0, True)
            with pool.Fori(1, HEADS // 2) as i:
                for u in range(2):
                    pre(2 * i + u, u)
                    v_copy(2 * i + (u - 1))
            v_copy(HEADS - 1)
            power(8, TT * HEADS, P, rec_sb, 2 * HEADS, r_rs)
            power(2, TT, D, n_sq[1], TT, n_rs[1])
            power(4, TT, D, n_sq[2], TT, n_rs[2])
            power(24, TT, D, f_sq, TT, f_rs)

        @block.scalar
        def _(act):
            def hi(i, base, s):
                act.wait_ge(raw_in[s % RAW], 16 * i + 16 * ((base + s) // RAW + 1))
                act.wait_ge(tile_done, RAW * i + (base + s + 1))
                act.copy(whi[:, s % HI, :], raw[:, s % RAW, :]).then_inc(hi_ready, 1)

            def norm(k):
                for t in range(TT):
                    if k == 0:
                        act.wait_ge(h_in[t], 16)
                    act.activation(hn[:, t, :], h[:, t, :], ACT.Square,
                                   accum_out=ss[:, 2 * k + t:2 * k + t + 1]).then_inc(n_sq[k], 1)
                for b in range(KC // 2):
                    act.wait_ge(n_tr[k], b + 1)
                    for c in (2 * b, 2 * b + 1):
                        m = act.activation(xh[:, c, :], ps[:, b, (c % 2) * S:(c % 2 + 1) * S], ACT.Copy,
                                           scale=gain[:, k, c:c + 1])
                    m.then_inc(n_xh[k], 1)

            def col_out(dst, bank, func, tiles):
                act.wait_ge(tile_done, tiles + HI)
                act.activation(dst, col_ps(bank), func).then_inc(col_free, 1)

            def cols(base, trips, dst, func, before):
                def body(i, prev):
                    for b in range(2):
                        hi(i, base, 2 * b)
                        hi(i, base, 2 * b + 1)
                        if prev is not None:
                            col_out(prev[0](i, b), b, prev[1], RAW * i + (base - RAW + COLT * (b + 1)))

                body(0, before)
                if trips > 1:
                    with act.Fori(1, trips) as i:
                        body(i, (lambda i, b: dst(2 * i + (b - 2)), func))

            def cols_end(dst, func, last, tiles):
                for b in range(2):
                    col_out(dst(last - 1 + b), b, func, tiles - COLT * (1 - b))

            act.wait_ge(lb_step, 3)
            act.activation(lb[:, 5:7, :], lb[:, 3:5, :], ACT.Exp).then_inc(lb_act, 1)
            norm(0)

            NF = HEADS // 2
            cols(A0, NF, lambda j: fg[:, j, :], ACT.Sigmoid, None)
            cols(A0 + NF * RAW, NF, lambda j: qq[:, j, :], ACT.Silu,
                 (lambda i, b: fg[:, HEADS - 2 + b, :], ACT.Sigmoid))
            cols_end(lambda j: qq[:, j, :], ACT.Silu, HEADS - 1, B0)

            def grp_out(n):
                act.wait_ge(tile_done, B0 + (n + 1) * GRPT + HI)
                for t in range(TT):
                    act.activation(tokens(n // 2)[:, t, n % 2 * GRP:(n % 2 + 1) * GRP], ps[:, 2 + 2 * (n % 2) + t, :],
                                   ACT.Silu if n // 2 == 1 else ACT.Copy).then_inc(grp_free, 1)

            for n in range(B_GRPS):
                for s in range(GRPT):
                    hi(2 * n, B0, s)
                    if s == HI - 1 and n:
                        grp_out(n - 1)
                    if n == 1 and s == HI:
                        act.wait_ge(f_ready, 1)
                        act.activation(bsum, bsum, ACT.Ln).then_inc(logf_ready, 1)
            hi(0, D0, 0)
            hi(0, D0, 1)
            grp_out(B_GRPS - 1)

            def attention_hi(j):
                k = slice(j * HEADS // 2, (j + 1) * HEADS // 2)
                act.wait_ge(att_sb, (j + 1) * HEADS // 2)
                act.wait_ge(tile_done, E0 + HI)
                act.copy(xh[:, k, :], att[:, k, :]).then_inc(att_hi, 1)

            def d_body(i, u, first=False, last=False):
                hd = 2 * i + u
                if not first:
                    act.wait_ge(tile_done, 2 * COLT * hd + (D0 + HI))
                    act.copy(qk[:, 2 * (1 - u) + 1, :], col_ps(1)).then_inc(col_free, 1)
                    act.wait_ge(min_ready, hd)
                    for t in range(TT):
                        r = slice(0, P) if t == 0 else slice(P, 3 * P)
                        act.activation(pr[:, r], pr[:, r], ACT.Exp, scale=-1.0, bias=small[:, t:t + 1],
                                       accum_out=small[:, 2 + t:3 + t]).then_inc(exp_ready, 1)
                hi(2 * i, D0, 4 * u + 2)
                hi(2 * i, D0, 4 * u + 3)
                if not last:
                    act.wait_ge(tile_done, 2 * COLT * hd + (D0 + COLT + HI))
                    act.copy(qk[:, 2 * u, :], col_ps(0)).then_inc(col_free, 1)
                    act.wait_ge(d_ready, hd + 1)
                    act.activation(E, E, ACT.Exp).then_inc(e_ready, 1)
                else:
                    attention_hi(0)
                if not first:
                    act.wait_ge(a_full, 2 * hd - 1)
                    act.copy(a01, ps[:, 7, 3 * P:4 * P]).then_inc(ax_ready, 1)
                    act.wait_ge(pt_full, hd)
                    act.copy(pT, ps[:, 7, 0:3 * P]).then_inc(pt_sb, 1)
                if not last:
                    hi(2 * i, D0, 4 * u + 4)
                    hi(2 * i, D0, 4 * u + 5)
                if not first:
                    act.wait_ge(o_full, hd)
                    act.copy(att[:, bass.DynSlice(hd - 1, 1), :].rearrange("p a b -> p (a b)"),
                             ps[:, 2, 0:S]).then_inc(att_sb, 1)
                    act.copy(orec[:, :, bass.DynSlice((hd - 1) * P, P)],
                             ps[:, 3, 0:S].rearrange("p (t c) -> p t c", t=TT)).then_inc(rec_sb, 1)
                    for t in range(TT):
                        sq = act.activation(junk[:, t, :], ps[:, 3, t * P:(t + 1) * P], ACT.Square,
                                            accum_out=ss[:, bass.DynSlice(hd + (7 + t * HEADS), 1)])
                    sq.then_inc(rec_sb, 1)

            d_body(0, 0, first=True)
            d_body(0, 1)
            with act.Fori(1, HEADS // 2) as i:
                d_body(i, 0)
                d_body(i, 1)
            d_body(HEADS // 2, 0, last=True)
            attention_hi(1)

            hi(0, E0, 4)
            hi(0, E0, 5)
            hi(0, E0, 6)
            for b in range(HEADS // 2):
                act.wait_ge(r_tr, b + 1)
                act.copy(xh[:, HEADS + 2 * b:HEADS + 2 * b + 2, :].rearrange("p a b -> p (a b)"),
                         ps[:, R_BANKS[b], :]).then_inc(r_hi, 1)
                if b == 0:
                    hi(0, E0, 7)
            with act.Fori(GRPT // RAW, (F0 - E0) // RAW) as i:
                for s in range(RAW):
                    hi(i, E0, s)
            act.wait_ge(grp_free, TT * GW)
            norm(1)

            cols(F0, PH, lambda j: qT[:, j, :], ACT.Copy, None)
            cols_end(lambda j: qT[:, j, :], ACT.Copy, 2 * PH - 1, G0)
            for b in range(8):
                act.wait_ge(sc_full, b + 1)
                act.copy(sc[:, 4 * b:4 * b + 4, :].rearrange("p a b -> p (a b)"), ps[:, b, :]).then_inc(sc_sb, 1)

            act.wait_ge(spilled, 16)
            act.wait_ge(sc_full, 8)
            cols(G0, GT0, lambda j: coef[:, j, :], ACT.Gelu, None)

            def spill_out(j, b):
                act.wait_ge(tile_done, RAW * j + (G0 + COLT * (b + 1) + HI))
                if not (isinstance(j, int) and j == GT0):
                    act.wait_ge(g_out[b], 16 * j - 16 * GT0)
                act.activation(stage[:, b, :], col_ps(b), ACT.Gelu).then_inc(col_free, 1)
                act.wait_ge(col_free, 2 * j + (CG + b + 1))
                act.dma_start(g_spill[2 * j + (b - DIRECT)], stage[:, b, :]).then_inc(g_out[b], 16)

            def prefill(g, u):
                act.wait_ge(gm_full, g + 1)
                act.copy(coef_t[:, bass.DynSlice(GATED * g, GATED), DIRECT:],
                         ps[:, 5 + u, :].rearrange("p (t e) -> p t e", t=GATED)[:, :, DIRECT:]).then_inc(g_pre, 1)

            hi(GT0, G0, 0)
            hi(GT0, G0, 1)
            col_out(coef[:, DIRECT - 2, :], 0, ACT.Gelu, RAW * GT0 + G0 - COLT)
            hi(GT0, G0, 2)
            hi(GT0, G0, 3)
            col_out(coef[:, DIRECT - 1, :], 1, ACT.Gelu, RAW * GT0 + G0)
            act.wait_ge(routed, TT * PH)
            act.activation(best, best, ACT.Exp).then_inc(gexp, 1)
            hi(GT0 + 1, G0, 0)
            hi(GT0 + 1, G0, 1)
            spill_out(GT0, 0)
            hi(GT0 + 1, G0, 2)
            hi(GT0 + 1, G0, 3)
            spill_out(GT0, 1)
            for j in range(3):
                act.wait_ge(it_full, j + 1)
                act.copy(slotT[:, j, :], ps[:, 2 + j, 0:S]).then_inc(it_sb, 1)

            def gate_trip(k, first=False):
                j = k + (GT0 + 2)
                hi(j, G0, 0)
                hi(j, G0, 1)
                spill_out(j - 1, 0)
                if not first:
                    prefill(2 * k - 1, 1)
                hi(j, G0, 2)
                hi(j, G0, 3)
                spill_out(j - 1, 1)
                prefill(2 * k, 0)

            gate_trip(0, True)
            with act.Fori(1, GTRIPS) as k:
                gate_trip(k)
            spill_out(NK // 2 - 1, 0)
            prefill(2 * GTRIPS - 1, 1)
            spill_out(NK // 2 - 1, 1)
            for g in range(2 * GTRIPS, S // GATED):
                prefill(g, g % 2)

            def u_body(i, first=False, back=False):
                for v in range(2):
                    hi(i, U0, 2 * v)
                    act.wait_ge(tile_done, RAW * i + (U0 + 2 * v - 2 * COLT + COLT + HI))
                    if first and v == 0:
                        act.wait_ge(gm_mul, S // GATED)
                    if back:
                        act.wait_ge(c_mul, 2 * i + (v - DIRECT + 1))
                    act.copy(ch[:, v, :], coef[:, 2 * i + v, :]).then_inc(c_hi, 1)
                    hi(i, U0, 2 * v + 1)

            u_body(0, first=True)
            with act.Fori(1, GT0) as i:
                u_body(i)
            with act.Fori(GT0, NK // 2) as i:
                u_body(i, back=True)
            act.wait_ge(h_up, 8)
            norm(2)

            def gate_out(i, j):
                act.wait_ge(tile_done, W0 + (2 * i + j + 1) * GRPT + HI)
                for t in range(TT):
                    act.activation(sgate[:, 2 * j + t, :], ps[:, 2 + 2 * j + t, :], ACT.Sigmoid).then_inc(w_sig, 1)

            for i in range(W_GRPS // 2):
                for j in range(2):
                    for s in range(GRPT):
                        hi(4 * i, W0, j * GRPT + s)
                        if s == HI - 1 and (i, j) != (0, 0):
                            gate_out(*((i, 0) if j else (i - 1, 1)))
            gate_out(W_GRPS // 2 - 1, 1)
            for t in range(TT):
                act.wait_ge(w_add, TT * W_GRPS)
                act.activation(hn[:, t, :], h[:, t, :], ACT.Square,
                               accum_out=ss[:, 24 + t:25 + t]).then_inc(f_sq, 1)

        @block.vector
        def _(dve):
            def lo(i, base, s):
                dve.wait_ge(hi_ready, RAW * i + (base + s + 1))
                dve.wait_ge(tile_done, RAW * i + (base + s + 1 - LO + HI))
                dve.tensor_tensor(wlo[:, s % LO, :], raw[:, s % RAW, :], whi[:, s % HI, :].bitcast(F32),
                                  ALU.subtract).then_inc(lo_ready, 1)

            def los(base, tiles):
                with dve.Fori(0, tiles // RAW) as i:
                    for s in range(RAW):
                        lo(i, base, s)

            def norm(k):
                dve.wait_ge(n_rs[k], 1)
                for t in range(TT):
                    dve.tensor_scalar(hn[:, t, :], h[:, t, :], rstd[:, 2 * k + t:2 * k + t + 1], None,
                                      ALU.mult).then_inc(n_row[k], 1)
                for b in range(KC // 2):
                    dve.wait_ge(n_xh[k], b + 1)
                    for c in (2 * b, 2 * b + 1):
                        m = dve.scalar_tensor_tensor(out=xl[:, c, :], in0=ps[:, b, (c % 2) * S:(c % 2 + 1) * S],
                                                     scalar=gain[:, k, c:c + 1], in1=xh[:, c, :].bitcast(F32),
                                                     op0=ALU.mult, op1=ALU.subtract)
                    m.then_inc(n_xl[k], 1)

            class Chain:

                def __init__(self, step):
                    self.step, self.base, self.n = step, 0, 0

                def start(self, base):
                    self.base, self.n = base, 0

                def mark(self, ins):
                    ins.then_inc(self.step, 1)
                    self.n += 1

                def sync(self):
                    dve.wait_ge(self.step, self.base + self.n)

                def link(self, ins):
                    self.mark(ins)
                    self.sync()

            c = Chain(lb_step)
            dve.wait_ge(const_in, 48)
            c.link(dve.tensor_tensor(lb[:, 2, :], lb[:, 0, :], lb[:, 1, :], ALU.max))
            dve.tensor_tensor(lb[:, 3, :], lb[:, 0, :], lb[:, 2, :], ALU.subtract).then_inc(lb_step, 1)
            dve.tensor_tensor(lb[:, 4, :], lb[:, 1, :], lb[:, 2, :], ALU.subtract).then_inc(lb_step, 1)
            c.n += 2
            dve.wait_ge(lb_act, 1)
            c.link(dve.tensor_tensor(lb[:, 7, :], lb[:, 5, :], lb[:, 6, :], ALU.add))
            c.link(dve.reciprocal(lb[:, 2, :], lb[:, 7, :]))
            c.link(dve.tensor_tensor(lb[:, 0, :], lb[:, 5, :], lb[:, 2, :], ALU.mult))
            c.link(dve.tensor_scalar(lb[:, 1, :], lb[:, 0, :], -1.0, 1.0, ALU.mult, ALU.add))
            norm(0)
            los(A0, B0 - A0)
            los(B0, RAW)
            dve.wait_ge(col_free, HEADS)
            for k in range(HEADS):
                m = dve.tensor_scalar(fg[:, k, :], fg[:, k, :], lb[:, 1, k:k + 1], lb[:, 0, k:k + 1], ALU.mult, ALU.add)
            m.then_inc(f_step, 1)
            los(B0 + RAW, RAW)
            dve.wait_ge(f_step, 1)
            dve.tensor_scalar(bsum, fg, TINY, None, ALU.max).then_inc(f_ready, 1)
            los(B0 + 2 * RAW, 4 * RAW)
            dve.wait_ge(mask_in, 48)
            dve.wait_ge(logf_ready, 1)
            for k in range(HEADS):
                m = dve.tensor_tensor_scan(bsum[:, k, :], ones, bsum[:, k, :], 0.0, ALU.mult, ALU.add)
            m.then_inc(b_ready, 1)
            los(B0 + 6 * RAW, D0 - B0 - 6 * RAW)
            lo(0, D0, 0)

            def attention_lo(j):
                k = slice(j * HEADS // 2, (j + 1) * HEADS // 2)
                dve.wait_ge(att_hi, j + 1)
                dve.tensor_tensor(xl[:, k, :], att[:, k, :], xh[:, k, :].bitcast(F32), ALU.subtract).then_inc(att_lo, 1)

            soft, mid = Chain(soft_step), Chain(mid_step)
            SOFT, MID = 2, 2

            def d_body(i, u, first=False, last=False):
                hd = 2 * i + u
                lo(2 * i, D0, 4 * u + 1)
                if not first:
                    soft.start((hd - 1) * SOFT)
                    dve.wait_ge(s_full, hd)
                    soft.link(dve.scalar_tensor_tensor(out=pr, in0=ps[:, 2, 0:3 * P], scalar=-SCALE, in1=cmask,
                                                       op0=ALU.mult, op1=ALU.add))
                    dve.tensor_reduce(small[:, 0:1], pr[:, 0:P], AX, ALU.min)
                    dve.tensor_reduce(small[:, 1:2], pr[:, P:3 * P], AX, ALU.min).then_inc(min_ready, 1)
                if not last:
                    lo(2 * i, D0, 4 * u + 2)
                if not first:
                    dve.wait_ge(exp_ready, 2 * hd)
                    soft.link(dve.reciprocal(small[:, 4:6], small[:, 2:4]))
                    dve.tensor_scalar(pr[:, 0:P], pr[:, 0:P], small[:, 4:5], None, ALU.mult)
                    dve.tensor_scalar(pr[:, P:3 * P], pr[:, P:3 * P], small[:, 5:6], None,
                                      ALU.mult).then_inc(p_ready, 1)
                if not last:
                    lo(2 * i, D0, 4 * u + 3)
                else:
                    attention_lo(0)
                if not first:
                    mid.start((hd - 1) * MID)
                    for t, a in ((0, a00), (1, a11)):
                        dve.wait_ge(a_full, 2 * hd - 1 + t)
                        if not (isinstance(hd, int) and hd == 1 and t == 0):
                            dve.wait_ge(a_ready, 2 * hd - 2 + t)
                        mid.link(dve.tensor_tensor(amask.rearrange("p a b -> p (a b)"),
                                                   ps[:, 3 + 2 * t:5 + 2 * t, :].rearrange("p a b -> p (a b)"),
                                                   masks.rearrange("p a b -> p (a b)"), ALU.mult))
                        r = dve.tensor_reduce(a, amask.rearrange("p l t -> p t l"), AX, ALU.add)
                        r.then_inc(a_ready, 1)
                if not last:
                    lo(2 * i, D0, 4 * u + 4)
                if not last:
                    dve.wait_ge(e_ready, hd + 1)
                    dve.wait_ge(kk_ready, hd + 1)
                    qrow, f = (v[:, bass.DynSlice(hd, 1), :].rearrange("p a b -> p (a b)") for v in (qq, fg))
                    for l in range(NL):
                        ql, kl = halves(QL[:, u * NL + l, :], l), halves(KL[:, u * NL + l, :], l)
                        if l < NL - 1:
                            el = halves(E[:, l, :], l)
                            dve.tensor_tensor(ql[:, :, 1, :], halves(qrow, l)[:, :, 1, :], el[:, :, 1, :], ALU.mult)
                            dve.tensor_tensor(kl[:, :, 0, :], halves(kk[:, u, :], l)[:, :, 0, :], el[:, :, 0, :],
                                              ALU.mult)
                        else:
                            dve.tensor_tensor(ql[:, :, 1, :], halves(qrow, l)[:, :, 1, :], halves(f, l)[:, :, 1, :],
                                              ALU.mult)
                            dve.tensor_copy(kl[:, :, 0, :], halves(kk[:, u, :], l)[:, :, 0, :]).then_inc(qk_ready, 1)

            dve.wait_ge(zeroed, 1)
            d_body(0, 0, first=True)
            d_body(0, 1)
            with dve.Fori(1, HEADS // 2) as i:
                d_body(i, 0)
                d_body(i, 1)
            d_body(HEADS // 2, 0, last=True)
            attention_lo(1)
            lo(0, E0, 2)
            lo(0, E0, 3)
            dve.wait_ge(gain_g, TT)
            dve.wait_ge(r_rs, 1)
            for k in range(HEADS):
                for t in range(TT):
                    o = orec[:, t, k * P:(k + 1) * P]
                    m = dve.scalar_tensor_tensor(out=o, in0=o, scalar=rstd[:, 8 + t * HEADS + k:9 + t * HEADS + k],
                                                 in1=gs[:, t, k * P:(k + 1) * P], op0=ALU.mult, op1=ALU.mult)
                m.then_inc(r_row, 1)
            lo(0, E0, 4)
            lo(0, E0, 5)
            for b in range(HEADS // 2):
                dve.wait_ge(r_hi, b + 1)
                k = slice(HEADS + 2 * b, HEADS + 2 * b + 2)
                dve.tensor_tensor(xl[:, k, :].rearrange("p a b -> p (a b)"), ps[:, R_BANKS[b], :],
                                  xh[:, k, :].rearrange("p a b -> p (a b)").bitcast(F32),
                                  ALU.subtract).then_inc(r_lo, 1)

            def h_add(i, j):
                dve.wait_ge(tile_done, i * (2 * GRPT) + (E0 + (j + 1) * GRPT + HI))
                for t in range(TT):
                    dst = h[:, t, bass.DynSlice(i * (2 * GRP) + j * GRP, GRP)]
                    dve.tensor_tensor(dst, ps[:, 2 + 2 * j + t, :], dst, ALU.add).then_inc(grp_free, 1)

            def e_body(i, first):
                for j in range(2):
                    for s in range(GRPT - 2 if first and j == 0 else 0, GRPT):
                        lo(4 * i, E0, j * GRPT + s)
                        if s == LO - 1 and j:
                            h_add(i, 0)
                        elif s == LO - 1 and not first:
                            h_add(i - 1, 1)

            e_body(0, True)
            with dve.Fori(1, E_GRPS // 2) as i:
                e_body(i, False)
            h_add(E_GRPS // 2 - 1, 1)
            dve.wait_ge(grp_free, TT * GW)
            norm(1)
            los(F0, G0 - F0)

            rt = Chain(rt_step)
            ROUTE = 13

            def hold(k):
                dve.memset(small[:, k:k + 1], 0.0)

            def route(r):
                def split(s):
                    lo(ROUTE_TILES // RAW * r, G0, s)

                rt.start(r * ROUTE)
                split(0)
                dve.wait_ge(routed, r)
                rt.mark(dve.tensor_scalar(sg, sc[:, bass.DynSlice(2 * r, 2), :], 1.0, None, ALU.mult))
                split(1)
                rt.sync()
                hold(0)
                for k in range(2):
                    m = dve.max(top[:, k, 0:8], sg[:, k, :])
                rt.mark(m)
                rt.sync()
                hold(1)
                for k in range(2):
                    dve.max_index(tixu[:, k, 0:8], top[:, k, 0:8], sg[:, k, :])
                    m = dve.match_replace(sg2[:, k, :], top[:, k, 0:8], sg[:, k, :], NEG)
                rt.mark(m)
                split(2)
                rt.sync()
                hold(2)
                for k in range(2):
                    m = dve.max(top[:, k, 8:TOP], sg2[:, k, :])
                rt.mark(m)
                rt.sync()
                hold(3)
                for k in range(2):
                    dve.max_index(tixu[:, k, 8:TOP], top[:, k, 8:TOP], sg2[:, k, :])
                rt.mark(dve.tensor_tensor(cand, top[:, 0, :].unsqueeze(2).to_broadcast([P, TOP, TOP]),
                                          top[:, 1, :].unsqueeze(1).to_broadcast([P, TOP, TOP]), ALU.add))
                split(3)
                rt.sync()
                cf, cf2 = (v.rearrange("p a b -> p (a b)") for v in (cand, cand2))
                dve.tensor_copy(tix, tixu)
                rt.mark(dve.max(bst[:, 0:8], cf))
                rt.sync()
                hold(4)
                dve.max_index(posu[:, 0:8], bst[:, 0:8], cf)
                rt.mark(dve.match_replace(cf2, bst[:, 0:8], cf, NEG))
                split(4)
                rt.sync()
                hold(5)
                rt.mark(dve.max(bst[:, 8:TOP], cf2))
                rt.sync()
                hold(6)
                rt.mark(dve.max_index(posu[:, 8:TOP], bst[:, 8:TOP], cf2))
                split(5)
                rt.sync()
                dve.tensor_scalar(best[:, r, :], bst, bst[:, 0:1], None, ALU.subtract)
                dve.tensor_scalar(abu[:, 0, :], posu, 4, None, ALU.logical_shift_right)
                rt.mark(dve.tensor_scalar(abu[:, 1, :], posu, TOP - 1, None, ALU.bitwise_and))
                rt.sync()
                rt.mark(dve.tensor_copy(ab, abu))
                split(6)
                rt.sync()
                ohf = oh.rearrange("p a b c -> p (a b) c")
                rt.mark(dve.tensor_tensor(ohf, ab.rearrange("p a b -> p (a b)").unsqueeze(2).to_broadcast([P, 2 * TOP, TOP]),
                                          iota[:, 0:TOP].unsqueeze(1).to_broadcast([P, 2 * TOP, TOP]), ALU.is_equal))
                split(7)
                rt.sync()
                for k in range(2):
                    m = dve.tensor_tensor(oh[:, k, :, :], oh[:, k, :, :],
                                          tix[:, k, :].unsqueeze(1).to_broadcast([P, TOP, TOP]), ALU.mult)
                rt.mark(m)
                rt.sync()
                assert rt.n == ROUTE
                dve.tensor_reduce(i1[:, r, :], oh[:, 0, :, :], AX, ALU.add)
                dve.tensor_reduce(i2[:, r, :], oh[:, 1, :, :], AX, ALU.add).then_inc(routed, 1)

            dve.wait_ge(sc_sb, 8)
            with dve.Fori(0, TT * PH) as r:
                route(r)
            lo(GT0, G0, 0)
            lo(GT0, G0, 1)
            gc = Chain(g_step)
            dve.wait_ge(gexp, 1)
            gc.link(dve.tensor_reduce(gsum, best, AX, ALU.add))
            gc.link(dve.reciprocal(gsum, gsum))
            dve.tensor_tensor(gate, best, gsum.unsqueeze(2).to_broadcast([P, TT * PH, TOP]), ALU.mult).then_inc(gates, 1)
            lo(GT0, G0, 2)
            lo(GT0, G0, 3)
            for t in range(RAW):
                lo(GT0 + 1, G0, t)

            def onehots(g, u):
                tk = slice(GATED * u, GATED * (u + 1))
                dve.tensor_tensor(oneL[:, tk, :],
                                  slotT[:, 0, bass.DynSlice(GATED * g, GATED)].unsqueeze(2).to_broadcast([P, GATED, P]),
                                  iota.unsqueeze(1).to_broadcast([P, GATED, P]), ALU.is_equal)
                for t in range(GATED):
                    m = dve.tensor_scalar(gateR[:, GATED * u + t, :], iota,
                                          slotT[:, 1, bass.DynSlice(GATED * g + t, 1)],
                                          slotT[:, 2, bass.DynSlice(GATED * g + t, 1)], ALU.is_equal, ALU.mult)
                m.then_inc(oh_ready, 1)

            def apply(g, u):
                dve.wait_ge(g_pre, g + 1)
                dst = coef_t[:, bass.DynSlice(GATED * g, GATED), 0:DIRECT]
                dve.tensor_tensor(dst, dst, ps[:, 5 + u, :].rearrange("p (t e) -> p t e", t=GATED)[:, :, 0:DIRECT],
                                  ALU.mult).then_inc(gm_mul, 1)

            def gate_trip(k, first=False):
                j = k + (GT0 + 2)
                lo(j, G0, 0)
                if first:
                    dve.wait_ge(it_sb, 3)
                onehots(2 * k, 0)
                lo(j, G0, 1)
                if not first:
                    apply(2 * k - 1, 1)
                lo(j, G0, 2)
                onehots(2 * k + 1, 1)
                lo(j, G0, 3)
                apply(2 * k, 0)

            gate_trip(0, True)
            with dve.Fori(1, GTRIPS) as k:
                gate_trip(k)
            for g in range(2 * GTRIPS, S // GATED):
                onehots(g, g % 2)
                apply(g - 1, (g - 1) % 2)
            apply(S // GATED - 1, 1)

            def multiply(m, v):
                dve.wait_ge(st_in[v], 8 * m + (16 - 8 * v))
                dst = coef[:, bass.DynSlice(m + DIRECT, 1), :].rearrange("p a b -> p (a b)")
                dve.tensor_tensor(dst, dst, stage[:, v, :], ALU.mult).then_inc(c_mul, 1)

            def u_body(i, back=False, last=False):
                for v in range(2):
                    lo(i, U0, 2 * v)
                    if back and not (last and v == 1):
                        multiply(2 * i + (v + 1 - DIRECT), 1 - v)
                    dve.wait_ge(c_hi, 2 * i + (v + 1))
                    dve.tensor_tensor(cl[:, v, :], coef[:, 2 * i + v, :], ch[:, v, :].bitcast(F32),
                                      ALU.subtract).then_inc(c_lo, 1)
                    lo(i, U0, 2 * v + 1)

            with dve.Fori(0, GT0) as i:
                u_body(i)
            multiply(0, 0)
            with dve.Fori(GT0, NK // 2 - 1) as i:
                u_body(i, back=True)
            u_body(NK // 2 - 1, back=True, last=True)
            dve.wait_ge(h_back, 16)
            dve.wait_ge(tile_done, W0 + HI)
            for t in range(TT):
                for g in range(4):
                    dst = h[:, t, g * GRP:(g + 1) * GRP]
                    dve.tensor_tensor(dst, ps[:, 4 * t + g, :], dst, ALU.add).then_inc(h_up, 1)
            dve.wait_ge(h_up, 8)
            norm(2)

            def w_out(i, j):
                for t in range(TT):
                    n = TT * (2 * i + j) + t
                    dve.wait_ge(w_sig, n + 1)
                    if n >= 2 * TT:
                        dve.wait_ge(w_add, n - 2 * TT + 1)
                    dve.tensor_tensor(ple_m[:, 2 * j + t, :], ps[:, 6 * j + t, :], sgate[:, 2 * j + t, :],
                                      ALU.mult).then_inc(grp_free, 1)
                    dve.wait_ge(grp_free, TT * GW + n + 1)
                    dst = h[:, t, (2 * i + j) * GRP:(2 * i + j + 1) * GRP]
                    dve.tensor_tensor(dst, ple_m[:, 2 * j + t, :], dst, ALU.add).then_inc(w_add, 1)

            for i in range(W_GRPS // 2):
                for j in range(2):
                    for s in range(GRPT):
                        lo(4 * i, W0, j * GRPT + s)
                        if s == HI - 1 and (i, j) != (0, 0):
                            w_out(*((i, 0) if j else (i - 1, 1)))
            w_out(W_GRPS // 2 - 1, 1)
            dve.wait_ge(f_rs, 1)
            dve.wait_ge(ple_in, 48)
            for t in range(TT):
                dve.scalar_tensor_tensor(out=orow[:, t, :], in0=h[:, t, :], scalar=rstd[:, 24 + t:25 + t],
                                         in1=gf_row, op0=ALU.mult, op1=ALU.mult).then_inc(f_row, 1)

        @block.tensor
        def _(pe):
            def norm(k):
                pe.wait_ge(n_row[k], TT)
                if k == 0:
                    pe.wait_ge(const_in, 48)
                for c in range(KC):
                    for t in range(TT):
                        mm = pe.transpose(ps[:, c // 2, (c % 2) * S + t * P:(c % 2) * S + (t + 1) * P],
                                          hn[:, t, c * P:(c + 1) * P], ident)
                    if c % 2:
                        mm.then_inc(n_tr[k], 1)
                    if k == 0 and c == 0:
                        pe.sem_inc(tile_done, HI)
                pe.wait_ge(n_xl[k], KC // 2)

            def parts(s, width):
                return (w.rearrange("p (k c) -> p k c", c=width) for w in (whi[:, s % HI, :], wlo[:, s % LO, :]))

            def col_tile(i, base, s, bank, second, free=None):
                if free is not None:
                    pe.wait_ge(col_free, free)
                pe.wait_ge(lo_ready, RAW * i + (base + s + 1))
                wh, wl = parts(s, P)
                for k in range(KPC):
                    kc = second * KPC + k
                    pe.matmul(col_ps(bank), wh[:, k, :], xh[:, kc, :], start=(kc == 0), stop=False)
                    pe.matmul(col_ps(bank), wh[:, k, :], xl[:, kc, :], start=False, stop=False)
                    mm = pe.matmul(col_ps(bank), wl[:, k, :], xh[:, kc, :], start=False, stop=(kc == KC - 1))
                mm.then_inc(tile_done, 1)

            def cols(base, c0, trips, first=False):
                def body(i, free):
                    for s in range(RAW):
                        col_tile(i, base, s, s // COLT, s % COLT,
                                 2 * i + (c0 + s // COLT - 1) if free and s % COLT == 0 else None)

                if first:
                    body(0, False)
                with pe.Fori(1 if first else 0, trips) as i:
                    body(i, True)

            def grp_tile(i, base, s, kt, bank):
                pe.wait_ge(lo_ready, RAW * i + (base + s + 1))
                wh, wl = parts(s, GRP)
                for t in range(TT):
                    tk = slice(t * P, (t + 1) * P)
                    for k in range(KPG):
                        kc = kt * KPG + k
                        o = ps[:, bank + t, :]
                        pe.matmul(o, xh[:, kc, tk], wh[:, k, :], start=(kc == 0), stop=False)
                        pe.matmul(o, xl[:, kc, tk], wh[:, k, :], start=False, stop=False)
                        mm = pe.matmul(o, xh[:, kc, tk], wl[:, k, :], start=False, stop=(kc == KC - 1))
                mm.then_inc(tile_done, 1)

            def groups(base, g0, pairs, first=False, start=0, extra=None):
                def body(i, free):
                    for j in range(2):
                        if free:
                            pe.wait_ge(grp_free, TT * 2 * i + TT * (g0 + j - 1))
                        if extra is not None:
                            extra(i, j)
                        for s in range(GRPT):
                            grp_tile(4 * i, base, j * GRPT + s, s, 2 + 2 * j)

                if first:
                    body(0, False)
                with pe.Fori(1 if first else start, pairs) as i:
                    body(i, True)

            norm(0)
            cols(A0, CA, A_COLS // 2, first=True)
            groups(B0, GB, B_GRPS // 2, first=True)

            def d_body(i, u, first=False, last=False):
                hd = 2 * i + u
                v = 1 - u
                if not last:
                    col_tile(2 * i, D0, 4 * u, 0, 0, 2 * hd + (CD - 1))
                if not first:
                    pe.wait_ge(col_free, 2 * hd + CD)
                    if isinstance(hd, int) and hd == 1:
                        pe.wait_ge(grp_free, TT * B_GRPS)
                    else:
                        pe.wait_ge(att_sb, hd - 1)
                    q, k = qk[:, 2 * v, :], qk[:, 2 * v + 1, :]
                    pe.matmul(ps[:, 2, 0:P], q[:, 0:P], k[:, 0:P], start=True, stop=True)
                    pe.matmul(ps[:, 2, P:3 * P], q[:, P:S], k, start=True, stop=True).then_inc(s_full, 1)
                if not last:
                    col_tile(2 * i, D0, 4 * u + 1, 0, 1)
                if not first:
                    pe.wait_ge(qk_ready, hd)
                    if not (isinstance(hd, int) and hd == 1):
                        pe.wait_ge(rec_sb, 2 * hd - 2)
                    for t in range(TT):
                        tk = slice(t * P, (t + 1) * P)
                        if t == 0:
                            pe.matmul(ps[:, 7, 3 * P:4 * P], KL[:, v * NL, 0:P], QL[:, v * NL, P:S],
                                      start=True, stop=True)
                        for l in range(1, NL + 1):
                            o = ps[:, 3 + 2 * t + (l - 1) // 4, (l - 1) % 4 * P:((l - 1) % 4 + 1) * P]
                            if l < NL:
                                pe.matmul(o, KL[:, v * NL + l, tk], QL[:, v * NL + l, tk], start=True, stop=True)
                            else:
                                qd = qq[:, bass.DynSlice(hd - 1, 1), tk].rearrange("p a b -> p (a b)")
                                mm = pe.matmul(o, kk[:, v, tk], qd, start=True, stop=True)
                        mm.then_inc(a_full, 1)
                if not last:
                    col_tile(2 * i, D0, 4 * u + 2, 1, 0, 2 * hd + CD)
                if not first:
                    pe.wait_ge(ax_ready, hd)
                    pe.wait_ge(p_ready, hd)
                    for j in range(3):
                        mm = pe.transpose(ps[:, 7, j * P:(j + 1) * P], pr[:, j * P:(j + 1) * P], ident)
                    mm.then_inc(pt_full, 1)
                if not last:
                    col_tile(2 * i, D0, 4 * u + 3, 1, 1)
                if not first:
                    pe.wait_ge(pt_sb, hd)
                    pe.wait_ge(v_ready, hd)
                    pe.matmul(ps[:, 2, 0:P], vh[:, 0, :], pT[:, 0:P], start=True, stop=True)
                    pe.matmul(ps[:, 2, P:S], vh[:, 0, :], pT[:, P:S], start=True, stop=False)
                    pe.matmul(ps[:, 2, P:S], vh[:, 1, :], pT[:, S:3 * P], start=False, stop=True)
                    pe.wait_ge(a_ready, 2 * hd)
                    vr = [gi[:, t, bass.DynSlice((hd - 1) * P, P)] for t in range(TT)]
                    pe.matmul(ps[:, 3, 0:P], a00, vr[0], start=True, stop=True)
                    pe.matmul(ps[:, 3, P:S], a01, vr[0], start=True, stop=False)
                    pe.matmul(ps[:, 3, P:S], a11, vr[1], start=False, stop=True).then_inc(o_full, 1)

            d_body(0, 0, first=True)
            d_body(0, 1)
            with pe.Fori(1, HEADS // 2) as i:
                d_body(i, 0)
                d_body(i, 1)
            d_body(HEADS // 2, 0, last=True)

            for s in range(GRPT):
                if s == GRPT // 2:
                    for c in range(HEADS):
                        pe.wait_ge(r_row, c + 1)
                        for t in range(TT):
                            mm = pe.transpose(ps[:, R_BANKS[c // 2], (c % 2) * S + t * P:(c % 2) * S + (t + 1) * P],
                                              orec[:, t, c * P:(c + 1) * P], ident)
                        if c % 2:
                            mm.then_inc(r_tr, 1)
                if s < GRPT // 2:
                    pe.wait_ge(att_lo, s // 2 + 1)
                    if s == 0:
                        pe.wait_ge(rec_sb, 2 * HEADS)
                else:
                    pe.wait_ge(r_lo, s - GRPT // 2 + 1)
                grp_tile(0, E0, s, s, 2)
            for s in range(GRPT):
                grp_tile(0, E0, GRPT + s, s, 4)
            groups(E0, GE, E_GRPS // 2, start=1)
            norm(1)
            cols(F0, CF, PH)
            pe.wait_ge(sk_in, 16)
            pe.wait_ge(col_free, CG)
            for t in range(TT):
                for g in range(2 * PH):
                    n = t * 2 * PH + g
                    mm = pe.matmul(ps[:, n // 4, n % 4 * P:(n % 4 + 1) * P], qT[:, g, t * P:(t + 1) * P],
                                   sk[:, g, :], start=True, stop=True)
                    if n % 4 == 3:
                        mm.then_inc(sc_full, 1)
            pe.wait_ge(sc_sb, 2)
            cols(G0, CG, GT0 + 1)
            pe.wait_ge(gates, 1)
            pe.wait_ge(sc_sb, 8)
            for j, v in enumerate((i1, i2, gate)):
                flat = v.rearrange("p a b -> p (a b)")
                for t in range(TT):
                    mm = pe.transpose(ps[:, 2 + j, t * P:(t + 1) * P], flat[:, t * P:(t + 1) * P], ident)
                mm.then_inc(it_full, 1)

            def gate_products(g, u, first):
                pe.wait_ge(oh_ready, g + 1)
                if not first:
                    pe.wait_ge(gm_mul, g - 1)
                for t in range(GATED):
                    mm = pe.matmul(ps[:, 5 + u, t * P:(t + 1) * P], oneL[:, GATED * u + t, :],
                                   gateR[:, GATED * u + t, :], start=True, stop=True)
                mm.then_inc(gm_full, 1)

            def gate_trip(j, k=None, first=False):
                for s in range(RAW):
                    col_tile(j, G0, s, s // COLT, s % COLT, 2 * j + (CG + s // COLT - 1) if s % COLT == 0 else None)
                    if k is not None and s % COLT:
                        gate_products(2 * k + s // COLT, s // COLT, first)

            gate_trip(GT0 + 1)
            gate_trip(GT0 + 2, 0, True)
            with pe.Fori(1, GTRIPS) as k:
                gate_trip(k + (GT0 + 2), k)
            for g in range(2 * GTRIPS, S // GATED):
                gate_products(g, g % 2, False)

            def u_body(i, first=False, last=False):
                for s in range(RAW):
                    v, dh = s // 2, s % 2
                    if dh == 0:
                        pe.wait_ge(c_lo, 2 * i + (v + 1))
                    pe.wait_ge(lo_ready, RAW * i + (U0 + s + 1))
                    wh, wl = parts(s, GRP)
                    st, sp_ = first and v == 0, last and v == 1
                    for t in range(TT):
                        tk = slice(t * P, (t + 1) * P)
                        for k in range(2):
                            o = ps[:, 4 * t + 2 * dh + k, :]
                            pe.matmul(o, ch[:, v, tk], wh[:, k, :], start=st, stop=False)
                            pe.matmul(o, cl[:, v, tk], wh[:, k, :], start=False, stop=False)
                            mm = pe.matmul(o, ch[:, v, tk], wl[:, k, :], start=False, stop=sp_)
                    mm.then_inc(tile_done, 1)

            u_body(0, first=True)
            with pe.Fori(1, NK // 2 - 1) as i:
                u_body(i)
            u_body(NK // 2 - 1, last=True)
            norm(2)

            def embed(i, j):
                for t in range(TT):
                    for k in range(PK):
                        pe.matmul(ps[:, 6 * j + t, :], ple_p[:, k, t * P:(t + 1) * P],
                                  ple_w[:, k, bass.DynSlice(i * (2 * GRP) + j * GRP, GRP)],
                                  start=(k == 0), stop=(k == PK - 1))

            pe.wait_ge(ple_in, 48)
            groups(W0, GW, W_GRPS // 2, extra=embed)


_OUT = ((1, S, D), "float32")


def blocks_of_columns(w):
    n = w.shape[1] // P
    return w.reshape(COLT, KPC, P, n, P).transpose(3, 0, 2, 1, 4).reshape(n * COLT, P, TILE)


def groups_of_columns(w):
    n = w.shape[1] // GRP
    return w.reshape(GRPT, KPG, P, n, GRP).transpose(3, 0, 2, 1, 4).reshape(n * GRPT, P, TILE)


def kernel(x, p, norm_mix, w_in, lb_logits, hgrn_norm, w_out, norm_ffn, peer_query, peer_sub_keys, peer_down,
           peer_up, norm_ple, w_ple, w_ple_gate, norm_final):
    import concourse.bacc as bacc
    from concourse.bass_utils import run_bass_kernel_spmd

    x, p, w_in, w_out, wq, wg = (np.asarray(a) for a in (x, p, w_in, w_out, peer_query, w_ple_gate))
    aq, ak, av, gq, gf, gi, gg = (w_in[0][:, k * HW:(k + 1) * HW] for k in range(7))
    heads = [a[:, k * P:(k + 1) * P] for k in range(HEADS) for a in (aq, ak)]
    rows = np.arange(P)
    s, t = rows[:, None], rows[None, :]
    level = [(s // (2 * m) == t // (2 * m)) & (s % (2 * m) < m) & (t % (2 * m) >= m) for m in HALVES[1:]]
    level_masks = np.stack(level + [s == t], 1).reshape(P, NL * P).astype(np.float32)
    hide = np.where(t > s, np.float32(-NEG), np.float32(0))
    consts = np.concatenate([np.eye(P), np.tile(rows, (P, 1))], 1).astype(np.float32)
    mix_consts = np.concatenate([hide, np.zeros((P, P)), hide, np.ones((P, S))], 1).astype(np.float32)
    gains = np.stack([np.asarray(g).reshape(KC, P).T for g in (norm_mix, norm_ffn, norm_ple)], 1)
    arrays = {
        "x": x.reshape(S, D),
        "win_t": blocks_of_columns(np.concatenate([gf, gq] + heads, 1)),
        "win_n": groups_of_columns(np.concatenate([gi, gg, av], 1)),
        "wout": groups_of_columns(w_out[0]),
        "wq": blocks_of_columns(wq[0]),
        "down": np.asarray(peer_down).reshape(NK, NK, COLT, KPC, P).transpose(1, 2, 4, 3, 0).reshape(-1, P, TILE),
        "up": np.asarray(peer_up).reshape(NK, NK, D),
        "wgate": groups_of_columns(wg[0]),
        "gains": gains,
        "lbl": np.asarray(lb_logits).reshape(2, HEADS, P).transpose(2, 0, 1),
        "gain_h": np.asarray(hgrn_norm).reshape(HW),
        "gain_f": np.asarray(norm_final).reshape(D),
        "skt": np.asarray(peer_sub_keys).reshape(2 * PH, NK, P).transpose(2, 0, 1).reshape(P, 2 * PH * NK),
        "pt": p.reshape(S, PK, P).transpose(2, 1, 0).reshape(P, PK * S),
        "wple": np.asarray(w_ple).reshape(PK, P, D).transpose(1, 0, 2).reshape(P, PK * D),
        "consts": consts,
        "mix_consts": mix_consts,
        "level_masks": level_masks,
    }
    arrays = {f"in_{k}": np.ascontiguousarray(v) for k, v in arrays.items()}
    nc = bacc.Bacc("TRN2", target_bir_lowering=False, num_devices=1, dynamic_dma_scratch_size=1024)
    ins = {k: nc.dram_tensor(k, a.shape, mybir.dt.from_np(a.dtype), kind="ExternalInput").ap()
           for k, a in arrays.items()}
    o = nc.dram_tensor("out_0", [S, D], F32, kind="ExternalOutput").ap()
    ins["in_up"] = ins["in_up"].rearrange("a b d -> b a d")
    program(nc, out=o, **{k[3:]: v for k, v in ins.items()})
    r = run_bass_kernel_spmd(nc, [arrays], core_ids=[0])
    return r.results[0]["out_0"].reshape(_OUT[0])
```

```python
from contextlib import ExitStack

import numpy as np

import concourse.bass as bass
from concourse import mybir

F32 = mybir.dt.float32
F32R = mybir.dt.float32r
U32 = mybir.dt.uint32
ALU = mybir.AluOpType
ACT = mybir.ActivationFunctionType
AX = mybir.AxisListType.X

P = 128
D = 2048
S = 256
TT = S // P
KC = D // P
HEADS = 8
HW = HEADS * P
GRP = 512
TILE = 1024
RAW = 4
HI = 4
LO = 2
COLT = KC * P // TILE
GRPT = KC * GRP // TILE
KPC = TILE // P
KPG = TILE // GRP
HALVES = [128, 64, 32, 16, 8, 4, 2, 1]
NL = len(HALVES)
PH = 8
NK = 128
TOP = 16
ROUTE_TILES = 8
DIRECT = TT * PH * ROUTE_TILES // COLT
GATED = 4
GT0 = DIRECT // 2
GTRIPS = NK // 2 - GT0 - 1
PLE = 256
PK = PLE // P
EPS = 1e-6
SCALE = float(P) ** -0.5
NEG = -3.0e38
MISC = 2944
TINY = 2.0 ** -64

A_COLS, B_GRPS, D_COLS, E_GRPS, F_COLS, W_GRPS = 16, 6, 16, D // GRP, 2 * PH, D // GRP
A0 = 0
B0 = A0 + A_COLS * COLT
D0 = B0 + B_GRPS * GRPT
E0 = D0 + D_COLS * COLT
F0 = E0 + E_GRPS * GRPT
G0 = F0 + F_COLS * COLT
U0 = G0 + NK * COLT
W0 = U0 + NK * D // TILE
CA, CD, CF, CG = 0, A_COLS, A_COLS + D_COLS, A_COLS + D_COLS + F_COLS
R_BANKS = [2, 3, 6, 7]
ATT_PARTS = [(0, 6), (6, HEADS)]
E_BANKS = [0, 4, 2, 4]
GB, GE, GW = 0, B_GRPS, B_GRPS + E_GRPS


def program(nc, x, win_t, win_n, wout, wq, down, up, wgate, gains, lbl, gain_h, gain_f, skt, pt, wple,
            consts, mix_consts, level_masks, out):
    with ExitStack() as ctx:
        def sb(name, shape, dt=F32):
            return ctx.enter_context(nc.sbuf_tensor(name, shape, dt))

        def sem(name):
            return ctx.enter_context(nc.semaphore(name))

        h_spill = nc.dram_tensor("h_spill", [P, TT, D], F32, kind="Internal").ap()
        g_spill = nc.dram_tensor("g_spill", [NK - DIRECT, P, S], F32, kind="Internal").ap()

        arena = sb("arena", [P, NK * S])
        raw = sb("raw", [P, RAW, TILE])
        whi = sb("whi", [P, HI, TILE], F32R)
        wlo = sb("wlo", [P, LO, TILE], F32R)
        xh = sb("xh", [P, KC, S], F32R)
        xl = sb("xl", [P, KC, S], F32R)
        cst = sb("cst", [P, 2 * P])
        gain = sb("gain", [P, 3, KC])
        ss = sb("ss", [P, 32])
        rstd = sb("rstd", [P, 32])
        half = sb("half", [P, 16])
        lb = sb("lb", [P, 8, HEADS])
        small = sb("small", [P, 8])
        part = sb("part", [P, TT, 4])
        ch = sb("ch", [P, 2, S], F32R)
        cl = sb("cl", [P, 2, S], F32R)
        misc = sb("misc", [P, MISC])
        stage = sb("stage", [P, 2, S])

        def view(of, base, shape):
            v = of[:, base:base + int(np.prod(shape))]
            names = "abc"[:len(shape)]
            return v if len(shape) == 1 else v.rearrange(
                f"p ({' '.join(names)}) -> p {' '.join(names)}", **dict(zip(names, shape)))

        ident, iota = cst[:, 0:P], cst[:, P:2 * P]

        at = {"arena": 0, "misc": 0}

        def take(*shape, of="arena"):
            v = view(arena if of == "arena" else misc, at[of], shape)
            at[of] += int(np.prod(shape))
            return v

        h = take(TT, D)
        hn = view(arena, at["arena"], (TT, D))
        fg = take(HEADS, S)
        qq = take(HEADS, S)
        take(B_GRPS // 2, TT, HW)
        tok = arena[:, at["arena"] - B_GRPS // 2 * TT * HW:at["arena"]]

        def tokens(which):
            return tok[:, which * TT * HW:(which + 1) * TT * HW].rearrange("p (t c) -> p t c", t=TT)

        gi, gs, va = tokens(0), tokens(1), tokens(2)
        orec = take(TT, HW)
        grow = orec[:, 0, :]
        QL_AT = at["arena"]
        QL, KL = take(2 * NL, S), take(2 * NL, S)
        E = take(NL - 1, S)
        masks = take(NL, P)
        amask = take(NL, P)
        a00, a01, a11 = take(P), take(P), take(P)
        mix_c = take(3 * P + S)
        cmask, ones = mix_c[:, 0:3 * P], mix_c[:, 3 * P:]
        qk = take(4, S)
        att = take(HEADS, S)
        bsum = att
        assert at["arena"] <= NK * S
        kk = take(2, S, of="misc")
        pr = take(3 * P, of="misc")
        pT = take(3 * P, of="misc")
        vh = take(2, P, of="misc")
        junk = take(2, P, of="misc")
        assert at["misc"] <= MISC
        sk = view(arena, 8192, (2 * PH, NK))
        qT = view(arena, 10240, (2 * PH, S))
        SC_AT = NK * S - TT * 2 * PH * NK
        sc = view(arena, SC_AT, (TT * 2 * PH, NK))
        at["misc"] = 0
        i1, i2, best, gate = (take(TT * PH, TOP, of="misc") for _ in range(4))
        R = at["misc"]
        sg, sg2 = take(2, NK, of="misc"), take(2, NK, of="misc")
        top, tixu, tix = take(2, TOP, of="misc"), take(2, TOP, of="misc").bitcast(U32), take(2, TOP, of="misc")
        cand, cand2 = take(TOP, TOP, of="misc"), take(TOP, TOP, of="misc")
        bst, posu = take(TOP, of="misc"), take(TOP, of="misc").bitcast(U32)
        abu, ab = take(2, TOP, of="misc").bitcast(U32), take(2, TOP, of="misc")
        oh = take(2, TOP, TOP, of="misc")
        isel = take(2, TOP, of="misc")
        gsum = take(TT * PH, of="misc")
        assert at["misc"] <= MISC
        at["misc"] = R
        slotT = take(3, S, of="misc")
        gateR = take(2 * GATED, P, of="misc")
        oneL = view(misc, 0, (2 * GATED, P))
        assert at["misc"] <= MISC and 2 * GATED * P <= R
        coef = view(arena, 0, (NK, S))
        coef_t = arena[:, :].rearrange("p (e t) -> p t e", t=S)
        ple_w = view(arena, 8192, (PK, D))
        ple_p = view(arena, 12288, (PK, S))
        gf_row = view(arena, 12800, (D,))
        BACK_TILES = (12800 + D) // S
        sgate = view(arena, 16384, (2 * TT, GRP))
        ple_m = view(arena, 18432, (2 * TT, GRP))
        orow = view(arena, 20480, (TT, D))

        ps = ctx.enter_context(nc.psum_tensor("ps", [P, 8, 512], F32))

        def col_ps(bank):
            return ps[:, bank, 0:S]

        const_in = sem("const_in")
        mask_in = sem("mask_in")
        h_in = [sem(f"h_in{t}") for t in range(TT)]
        raw_in = [sem(f"raw_in{i}") for i in range(RAW)]
        hi_ready, lo_ready, tile_done = sem("hi_ready"), sem("lo_ready"), sem("tile_done")
        col_free = sem("col_free")
        grp_free = sem("grp_free")
        lb_step, lb_act = sem("lb_step"), sem("lb_act")
        NORMS = ["mix", "ffn", "ple", "final"]
        n_part, n_sq, n_rs = ([sem(f"n_{what}_{n}") for n in NORMS] for what in ("part", "sq", "rs"))
        n_row0, n_row1, n_tr, n_xh, n_xl = (
            [sem(f"n_{what}_{n}") for n in NORMS[:3]] for what in ("row0", "row1", "tr", "xh", "xl"))
        pool_step, zeroed = sem("pool_step"), sem("zeroed")
        gain_g = sem("gain_g")
        f_step, f_ready, logf_ready, b_ready = (sem(n) for n in ("f_step", "f_ready", "logf_ready", "b_ready"))
        kk_ready, d_ready, e_ready, qk_ready = (sem(n) for n in ("kk_ready", "d_ready", "e_ready", "qk_ready"))
        soft_step, mid_step = sem("soft_step"), sem("mid_step")
        s_full, min_ready, exp_ready, p_ready = (sem(n) for n in ("s_full", "min_ready", "exp_ready", "p_ready"))
        a_full, a_ready, ax_ready = sem("a_full"), sem("a_ready"), sem("ax_ready")
        pt_full, pt_sb, v_ready = sem("pt_full"), sem("pt_sb"), sem("v_ready")
        o_full, att_sb, rec_sb = sem("o_full"), sem("att_sb"), sem("rec_sb")
        att_hi, att_lo = sem("att_hi"), sem("att_lo")
        r_rs, r_row, r_tr, r_hi, r_lo = (sem(f"r_{n}") for n in ("rs", "row", "tr", "hi", "lo"))
        spilled, sk_in, sc_full, sc_sb = sem("spilled"), sem("sk_in"), sem("sc_full"), sem("sc_sb")
        rt_step, routed, gexp, g_step, gates = (sem(n) for n in ("rt_step", "routed", "gexp", "g_step", "gates"))
        it_full, it_sb = sem("it_full"), sem("it_sb")
        oh_ready, gm_full, gm_mul = sem("oh_ready"), sem("gm_full"), sem("gm_mul")
        g_pre = sem("g_pre")
        g_out = [sem(f"g_out{b}") for b in range(2)]
        st_in = [sem(f"st_in{b}") for b in range(2)]
        c_mul, c_hi, c_lo = sem("c_mul"), sem("c_hi"), sem("c_lo")
        u_first = sem("u_first")
        h_back, h_up, ple_in = sem("h_back"), sem("h_up"), sem("ple_in")
        w_sig, w_add = sem("w_sig"), sem("w_add")
        f_gain, f_row, stored = sem("f_gain"), [sem(f"f_row{t}") for t in range(TT)], sem("stored")

        def halves(v, l):
            return v.rearrange("p (n two h) -> p n two h", two=2, h=HALVES[l])

        block = ctx.enter_context(nc.Block())

        @block.sync
        def _(sp):
            for t in range(TT):
                sp.dma_start(h[:, t, :], x[t * P:(t + 1) * P, :]).then_inc(h_in[t], 16)
            sp.dma_start(cst[:], consts).then_inc(const_in, 16)
            sp.dma_start(gain[:], gains).then_inc(const_in, 16)
            sp.dma_start(lb[:, 0:2, :], lbl).then_inc(const_in, 16)

            def load(src, s, split):
                if split is not None:
                    sp.wait_ge(lo_ready, split)
                sp.dma_start(raw[:, s, :], src).then_inc(raw_in[s], 16)

            def stream(src, base, tiles, first=0):
                with sp.Fori(0, tiles // RAW) as i:
                    for s in range(RAW):
                        load(src[RAW * i + (first + s)], s, RAW * i + (base + s - RAW + 1))

            for s in range(RAW):
                load(win_t[s], s, None)
            sp.dma_start(masks.rearrange("p a b -> p (a b)"), level_masks).then_inc(mask_in, 16)
            sp.dma_start(grow, gain_h.partition_broadcast(P)).then_inc(mask_in, 16)
            sp.dma_start(mix_c, mix_consts).then_inc(mask_in, 16)
            with sp.Fori(1, A_COLS * COLT // RAW) as i:
                for s in range(RAW):
                    load(win_t[RAW * i + s], s, RAW * i + (s - RAW + 1))
            stream(win_n, B0, D0 - B0)
            stream(win_t, D0, E0 - D0, A_COLS * COLT)
            stream(wout, E0, F0 - E0)

            def wq_tiles(i):
                for s in range(RAW):
                    load(wq[RAW * i + s], s, RAW * i + (F0 + s - RAW + 1))

            wq_tiles(0)
            sp.wait_ge(grp_free, TT * GW)
            sp.dma_start(sk.rearrange("p a b -> p (a b)"), skt).then_inc(sk_in, 16)
            for t in range(TT):
                wq_tiles(1 + t)
                sp.dma_start(h_spill[:, t, :], h[:, t, :]).then_inc(spilled, 16)
            with sp.Fori(1 + TT, (G0 - F0) // RAW) as i:
                wq_tiles(i)
            stream(down, G0, U0 - G0)

            def up_tiles(i, back=False, first=False):
                for s in range(RAW):
                    if back and s % COLT == 0:
                        v = s // COLT
                        if not first:
                            sp.wait_ge(c_mul, 2 * i + (v - DIRECT - 1))
                        sp.dma_start(stage[:, v, :], g_spill[2 * i + (v - DIRECT)]).then_inc(st_in[v], 16)
                    load(up[2 * i + s // 2, :, (s % 2) * TILE:(s % 2 + 1) * TILE], s,
                         RAW * i + (U0 + s - RAW + 1))

            with sp.Fori(0, GT0) as i:
                up_tiles(i)
            for b in range(2):
                sp.wait_ge(g_out[b], 16 * (NK - DIRECT) // 2)
            up_tiles(GT0, back=True, first=True)
            sp.wait_ge(c_lo, BACK_TILES)
            back = [(h[:, t, :], h_spill[:, t, :], h_back) for t in range(TT)]
            back += [(ple_w[:, k, :], wple[:, k, :], ple_in) for k in range(PK)]
            back += [(ple_p, pt, ple_in), (gf_row, gain_f.partition_broadcast(P), ple_in)]
            for i, (dst, src, landed) in enumerate(back):
                sp.dma_start(dst, src).then_inc(landed, 16)
                up_tiles(GT0 + 1 + i, back=True)
            with sp.Fori(GT0 + 1 + len(back), NK // 2) as i:
                up_tiles(i, back=True)
            stream(wgate, W0, W_GRPS * GRPT)
            for half_ in range(2):
                for t in range(TT):
                    sp.wait_ge(f_row[t], half_ + 1)
                    c = slice(half_ * D // 2, (half_ + 1) * D // 2)
                    sp.dma_start(out[t * P:(t + 1) * P, c], orow[:, t, c]).then_inc(stored, 16)
            sp.wait_ge(stored, 16 * 2 * TT)

        @block.gpsimd
        def _(pool):
            steps = 0

            def power(first, width, count, ready, need, done):
                nonlocal steps
                v = ss[:, first:first + width]
                pool.wait_ge(ready, need)
                pool.tensor_scalar(v, v, 1.0 / count, EPS, ALU.mult, ALU.add).then_inc(pool_step, 1)
                steps += 1
                pool.wait_ge(pool_step, steps)
                pool.tensor_tensor(rstd[:, first:first + width], v, half[:, 0:width], ALU.pow).then_inc(done, 1)

            steps += 1
            pool.memset(half[:], -0.5).then_inc(pool_step, 1)
            for t in range(TT):
                power(t, 1, D, n_sq[0], t + 1, n_rs[0])
            pool.memset(arena[:, QL_AT:QL_AT + 4 * NL * S], 0.0).then_inc(zeroed, 1)
            pool.wait_ge(grp_free, TT * 4)
            pool.wait_ge(mask_in, 48)
            for t in range(TT):
                pool.tensor_tensor(gs[:, t, :], gs[:, t, :], grow, ALU.mult).then_inc(gain_g, 1)
            def pre(i, u, first=False):
                if not first:
                    pool.wait_ge(qk_ready, i)
                b = bsum[:, bass.DynSlice(i, 1), :].rearrange("p a b -> p (a b)")
                for l in range(NL - 1):
                    bl, el = halves(b, l), halves(E[:, l, :], l)
                    mid = bl[:, :, 0, HALVES[l] - 1:HALVES[l]].to_broadcast([P, S // 2 // HALVES[l], HALVES[l]])
                    pool.tensor_tensor(el[:, :, 1, :], bl[:, :, 1, :], mid, ALU.subtract)
                    d = pool.tensor_tensor(el[:, :, 0, :], mid, bl[:, :, 0, :], ALU.subtract)
                d.then_inc(d_ready, 1)
                if not (isinstance(i, int) and i < 2):
                    pool.wait_ge(a_full, 2 * i - 2)
                pool.tensor_tensor(kk[:, u, :], ones, fg[:, bass.DynSlice(i, 1), :].rearrange("p a b -> p (a b)"),
                                   ALU.subtract).then_inc(kk_ready, 1)

            def v_copy(i, first=False):
                if not first:
                    pool.wait_ge(o_full, i)
                pool.tensor_copy(vh, va[:, :, bass.DynSlice(i * P, P)]).then_inc(v_ready, 1)

            pool.wait_ge(b_ready, 1)
            pre(0, 0, True)
            pre(1, 1)
            pool.wait_ge(grp_free, TT * B_GRPS)
            v_copy(0, True)
            with pool.Fori(1, HEADS // 2) as i:
                for u in range(2):
                    pre(2 * i + u, u)
                    v_copy(2 * i + (u - 1))
            v_copy(HEADS - 1)
            power(8, TT * HEADS, P, rec_sb, 2 * HEADS, r_rs)
            for k in (1, 2, 3):
                for t in range(TT):
                    power(2 * k + t, 1, D, n_sq[k], t + 1, n_rs[k])

        @block.scalar
        def _(act):
            def hi(i, base, s):
                act.wait_ge(raw_in[s % RAW], 16 * i + 16 * ((base + s) // RAW + 1))
                act.wait_ge(tile_done, RAW * i + (base + s + 1))
                act.copy(whi[:, s % HI, :], raw[:, s % RAW, :]).then_inc(hi_ready, 1)

            def square(k, t, g):
                act.activation(hn[:, t, g * GRP:(g + 1) * GRP], h[:, t, g * GRP:(g + 1) * GRP], ACT.Square,
                               accum_out=part[:, t, g:g + 1]).then_inc(n_part[k], 1)

            def norm(k, stage):
                hi(0, stage, 0)
                act.wait_ge(n_rs[k], TT)
                for c in range(2):
                    cols_ = slice(c * D // 2, (c + 1) * D // 2)
                    act.activation(hn[:, 1, cols_], h[:, 1, cols_], ACT.Copy,
                                   scale=rstd[:, 2 * k + 1:2 * k + 2]).then_inc(n_row1[k], 1)
                for b in range(KC // 2):
                    act.wait_ge(n_tr[k], b + 1)
                    for c in (2 * b, 2 * b + 1):
                        m = act.activation(xh[:, c, :], ps[:, b, (c % 2) * S:(c % 2 + 1) * S], ACT.Copy,
                                           scale=gain[:, k, c:c + 1])
                    m.then_inc(n_xh[k], 1)
                    if b == KC // 4:
                        hi(0, stage, 1)
                for s in range(2, HI):
                    hi(0, stage, s)

            def col_out(dst, bank, func, tiles):
                act.wait_ge(tile_done, tiles + HI)
                act.activation(dst, col_ps(bank), func).then_inc(col_free, 1)

            def cols(base, trips, dst, func, before, ahead=False):
                def body(i, prev, split=True):
                    for b in range(2):
                        if split:
                            hi(i, base, 2 * b)
                            hi(i, base, 2 * b + 1)
                        if prev is not None:
                            col_out(prev[0](i, b), b, prev[1], RAW * i + (base - RAW + COLT * (b + 1)))

                body(0, before, not ahead)
                if trips > 1:
                    with act.Fori(1, trips) as i:
                        body(i, (lambda i, b: dst(2 * i + (b - 2)), func))

            def cols_end(dst, func, last, tiles, split=False):
                for b in range(2):
                    if split:
                        hi(0, tiles, 2 * b)
                        hi(0, tiles, 2 * b + 1)
                    col_out(dst(last - 1 + b), b, func, tiles - COLT * (1 - b))

            for t in range(TT):
                act.wait_ge(h_in[t], 16)
                act.activation(hn[:, t, :], h[:, t, :], ACT.Square,
                               accum_out=ss[:, t:t + 1]).then_inc(n_sq[0], 1)
            act.wait_ge(lb_step, 3)
            act.activation(lb[:, 5:7, :], lb[:, 3:5, :], ACT.Exp).then_inc(lb_act, 1)
            norm(0, A0)

            NF = HEADS // 2
            cols(A0, NF, lambda j: fg[:, j, :], ACT.Sigmoid, None, ahead=True)
            cols(A0 + NF * RAW, NF, lambda j: qq[:, j, :], ACT.Silu,
                 (lambda i, b: fg[:, HEADS - 2 + b, :], ACT.Sigmoid))
            cols_end(lambda j: qq[:, j, :], ACT.Silu, HEADS - 1, B0, split=True)

            def grp_out(n):
                act.wait_ge(tile_done, B0 + (n + 1) * GRPT + HI)
                for t in range(TT):
                    act.activation(tokens(n // 2)[:, t, n % 2 * GRP:(n % 2 + 1) * GRP], ps[:, 2 + 2 * (n % 2) + t, :],
                                   ACT.Silu if n // 2 == 1 else ACT.Copy).then_inc(grp_free, 1)

            for n in range(B_GRPS):
                for s in range(GRPT):
                    if n or s >= HI:
                        hi(2 * n, B0, s)
                    if s == HI - 1 and n:
                        grp_out(n - 1)
                    if n == 1 and s == HI:
                        act.wait_ge(f_ready, 1)
                        act.activation(bsum, bsum, ACT.Ln).then_inc(logf_ready, 1)
            hi(0, D0, 0)
            hi(0, D0, 1)
            grp_out(B_GRPS - 1)

            def attention_hi(j):
                k = slice(*ATT_PARTS[j])
                act.wait_ge(att_sb, ATT_PARTS[j][1])
                act.wait_ge(tile_done, E0 + HI)
                act.copy(xh[:, k, :], att[:, k, :]).then_inc(att_hi, 1)

            def d_body(i, u, first=False, last=False):
                hd = 2 * i + u
                hi(2 * i, D0, 4 * u + 2)
                if not first:
                    act.wait_ge(tile_done, 2 * COLT * hd + (D0 + HI))
                    act.copy(qk[:, 2 * (1 - u) + 1, :], col_ps(1)).then_inc(col_free, 1)
                    if last:
                        attention_hi(0)
                    act.wait_ge(min_ready, hd)
                    for t in range(TT):
                        r = slice(0, P) if t == 0 else slice(P, 3 * P)
                        act.activation(pr[:, r], pr[:, r], ACT.Exp, scale=-1.0, bias=small[:, t:t + 1],
                                       accum_out=small[:, 2 + t:3 + t]).then_inc(exp_ready, 1)
                hi(2 * i, D0, 4 * u + 3)
                if not last:
                    act.wait_ge(tile_done, 2 * COLT * hd + (D0 + COLT + HI))
                    act.copy(qk[:, 2 * u, :], col_ps(0)).then_inc(col_free, 1)
                    act.wait_ge(d_ready, hd + 1)
                    act.activation(E, E, ACT.Exp).then_inc(e_ready, 1)
                if not first:
                    act.wait_ge(a_full, 2 * hd - 1)
                    act.copy(a01, ps[:, 7, 3 * P:4 * P]).then_inc(ax_ready, 1)
                if not last:
                    hi(2 * i, D0, 4 * u + 4)
                    hi(2 * i, D0, 4 * u + 5)
                if not first:
                    act.wait_ge(pt_full, hd)
                    act.copy(pT, ps[:, 7, 0:3 * P]).then_inc(pt_sb, 1)
                    act.wait_ge(o_full, hd)
                    act.copy(att[:, bass.DynSlice(hd - 1, 1), :].rearrange("p a b -> p (a b)"),
                             ps[:, 2, 0:S]).then_inc(att_sb, 1)
                    act.copy(orec[:, :, bass.DynSlice((hd - 1) * P, P)],
                             ps[:, 3, 0:S].rearrange("p (t c) -> p t c", t=TT)).then_inc(rec_sb, 1)
                    for t in range(TT):
                        sq = act.activation(junk[:, t, :], ps[:, 3, t * P:(t + 1) * P], ACT.Square,
                                            accum_out=ss[:, bass.DynSlice(hd + (7 + t * HEADS), 1)])
                    sq.then_inc(rec_sb, 1)

            d_body(0, 0, first=True)
            d_body(0, 1)
            with act.Fori(1, HEADS // 2) as i:
                d_body(i, 0)
                d_body(i, 1)
            d_body(HEADS // 2, 0, last=True)
            attention_hi(1)

            for s in range(HI, GRPT - 1):
                hi(0, E0, s)
            for b in range(HEADS // 2):
                act.wait_ge(r_tr, b + 1)
                act.copy(xh[:, HEADS + 2 * b:HEADS + 2 * b + 2, :].rearrange("p a b -> p (a b)"),
                         ps[:, R_BANKS[b], :]).then_inc(r_hi, 1)
                if b == 0:
                    hi(0, E0, GRPT - 1)
            def squares(n):
                for t in range(TT):
                    act.wait_ge(grp_free, TT * (GE + n) + t + 1)
                    square(1, t, n)

            for n in range(1, E_GRPS):
                for s in range(GRPT):
                    hi(2 * n, E0, s)
                    if s == HI:
                        squares(n - 1)
            squares(E_GRPS - 1)
            norm(1, F0)

            cols(F0, PH, lambda j: qT[:, j, :], ACT.Copy, None, ahead=True)
            cols_end(lambda j: qT[:, j, :], ACT.Copy, 2 * PH - 1, G0)
            for s in range(HI):
                hi(0, G0, s)
            for b in range(8):
                act.wait_ge(sc_full, b + 1)
                act.copy(sc[:, 4 * b:4 * b + 4, :].rearrange("p a b -> p (a b)"), ps[:, b, :]).then_inc(sc_sb, 1)

            act.wait_ge(spilled, 16 * TT)
            act.wait_ge(sc_full, 8)
            cols(G0, GT0, lambda j: coef[:, j, :], ACT.Gelu, None, ahead=True)

            def spill_out(j, b):
                act.wait_ge(tile_done, RAW * j + (G0 + COLT * (b + 1) + HI))
                if not (isinstance(j, int) and j == GT0):
                    act.wait_ge(g_out[b], 16 * j - 16 * GT0)
                act.activation(stage[:, b, :], col_ps(b), ACT.Gelu).then_inc(col_free, 1)
                act.wait_ge(col_free, 2 * j + (CG + b + 1))
                act.dma_start(g_spill[2 * j + (b - DIRECT)], stage[:, b, :]).then_inc(g_out[b], 16)

            def prefill(g, u):
                act.wait_ge(gm_full, g + 1)
                act.copy(coef_t[:, bass.DynSlice(GATED * g, GATED), DIRECT:],
                         ps[:, 5 + u, :].rearrange("p (t e) -> p t e", t=GATED)[:, :, DIRECT:]).then_inc(g_pre, 1)

            hi(GT0, G0, 0)
            hi(GT0, G0, 1)
            col_out(coef[:, DIRECT - 2, :], 0, ACT.Gelu, RAW * GT0 + G0 - COLT)
            hi(GT0, G0, 2)
            hi(GT0, G0, 3)
            col_out(coef[:, DIRECT - 1, :], 1, ACT.Gelu, RAW * GT0 + G0)
            act.wait_ge(routed, TT * PH)
            act.activation(best, best, ACT.Exp).then_inc(gexp, 1)
            hi(GT0 + 1, G0, 0)
            hi(GT0 + 1, G0, 1)
            spill_out(GT0, 0)
            hi(GT0 + 1, G0, 2)
            hi(GT0 + 1, G0, 3)
            spill_out(GT0, 1)
            for j in range(3):
                act.wait_ge(it_full, j + 1)
                act.copy(slotT[:, j, :], ps[:, 2 + j, 0:S]).then_inc(it_sb, 1)

            def gate_trip(k, first=False):
                j = k + (GT0 + 1)
                hi(j, G0, 0)
                hi(j, G0, 1)
                spill_out(j - 1, 0)
                if first:
                    prefill(0, 0)
                prefill(2 * k - 1, 1)
                hi(j, G0, 2)
                hi(j, G0, 3)
                spill_out(j - 1, 1)
                prefill(2 * k, 0)

            gate_trip(1, True)
            with act.Fori(2, GTRIPS) as k:
                gate_trip(k)
            hi(0, U0, 0)
            hi(0, U0, 1)
            spill_out(NK // 2 - 1, 0)
            prefill(2 * GTRIPS - 1, 1)
            hi(0, U0, 2)
            hi(0, U0, 3)
            spill_out(NK // 2 - 1, 1)
            for g in range(2 * GTRIPS, S // GATED):
                prefill(g, g % 2)

            def u_body(i, first=False, back=False):
                for v in range(2):
                    if not first:
                        hi(i, U0, 2 * v)
                    act.wait_ge(tile_done, RAW * i + (U0 + 2 * v - 2 * COLT + COLT + HI))
                    if first and v == 0:
                        act.wait_ge(gm_mul, S // GATED)
                    if back:
                        act.wait_ge(c_mul, 2 * i + (v - DIRECT + 1))
                    act.copy(ch[:, v, :], coef[:, 2 * i + v, :]).then_inc(c_hi, 1)
                    if not first:
                        hi(i, U0, 2 * v + 1)

            u_body(0, first=True)
            with act.Fori(1, GT0) as i:
                u_body(i)
            with act.Fori(GT0, NK // 2) as i:
                u_body(i, back=True)
            for t in range(TT):
                for g in range(4):
                    act.wait_ge(h_up, 4 * t + g + 1)
                    square(2, t, g)
            norm(2, W0)

            def gate_out(n):
                act.wait_ge(tile_done, W0 + (n + 1) * GRPT + HI)
                j = n % 2
                for t in range(TT):
                    act.activation(sgate[:, 2 * j + t, :], ps[:, 2 + 2 * j + t, :], ACT.Sigmoid).then_inc(w_sig, 1)

            def last_squares(n):
                for t in range(TT):
                    act.wait_ge(w_add, TT * n + t + 1)
                    square(3, t, n)

            for n in range(W_GRPS):
                for s in range(GRPT):
                    if n or s >= HI:
                        hi(2 * n, W0, s)
                    if n and s == HI - 1:
                        gate_out(n - 1)
                    if n and s == GRPT - 2:
                        last_squares(n - 1)
            gate_out(W_GRPS - 1)
            last_squares(W_GRPS - 1)
            act.wait_ge(n_rs[3], TT)
            act.wait_ge(f_gain, TT * W_GRPS)
            for c in range(2):
                o = orow[:, 1, c * D // 2:(c + 1) * D // 2]
                act.activation(o, o, ACT.Copy, scale=rstd[:, 7:8]).then_inc(f_row[1], 1)

        @block.vector
        def _(dve):
            def lo(i, base, s):
                dve.wait_ge(hi_ready, RAW * i + (base + s + 1))
                dve.wait_ge(tile_done, RAW * i + (base + s + 1 - LO + HI))
                dve.tensor_tensor(wlo[:, s % LO, :], raw[:, s % RAW, :], whi[:, s % HI, :].bitcast(F32),
                                  ALU.subtract).then_inc(lo_ready, 1)

            def los(base, tiles):
                with dve.Fori(0, tiles // RAW) as i:
                    for s in range(RAW):
                        lo(i, base, s)

            def row_sum(k, t):
                dve.wait_ge(n_part[k], (4 * t + 4) if k == 2 else TT * (E_GRPS - 1) + t + 1)
                dve.tensor_reduce(ss[:, 2 * k + t:2 * k + t + 1], part[:, t, :], AX, ALU.add).then_inc(n_sq[k], 1)

            def rows(k):
                dve.wait_ge(n_rs[k], 1)
                for c in range(2):
                    cols_ = slice(c * D // 2, (c + 1) * D // 2)
                    dve.tensor_scalar(hn[:, 0, cols_], h[:, 0, cols_], rstd[:, 2 * k:2 * k + 1], None,
                                      ALU.mult).then_inc(n_row0[k], 1)

            def norm(k, stage):
                for b in range(KC // 2):
                    dve.wait_ge(n_xh[k], b + 1)
                    for c in (2 * b, 2 * b + 1):
                        m = dve.scalar_tensor_tensor(out=xl[:, c, :], in0=ps[:, b, (c % 2) * S:(c % 2 + 1) * S],
                                                     scalar=gain[:, k, c:c + 1], in1=xh[:, c, :].bitcast(F32),
                                                     op0=ALU.mult, op1=ALU.subtract)
                    m.then_inc(n_xl[k], 1)
                    if b == KC // 4:
                        lo(0, stage, 1)

            class Chain:

                def __init__(self, step):
                    self.step, self.base, self.n = step, 0, 0

                def start(self, base):
                    self.base, self.n = base, 0

                def mark(self, ins):
                    ins.then_inc(self.step, 1)
                    self.n += 1

                def sync(self):
                    dve.wait_ge(self.step, self.base + self.n)

                def link(self, ins):
                    self.mark(ins)
                    self.sync()

            c = Chain(lb_step)
            dve.wait_ge(const_in, 48)
            c.link(dve.tensor_tensor(lb[:, 2, :], lb[:, 0, :], lb[:, 1, :], ALU.max))
            dve.tensor_tensor(lb[:, 3, :], lb[:, 0, :], lb[:, 2, :], ALU.subtract).then_inc(lb_step, 1)
            dve.tensor_tensor(lb[:, 4, :], lb[:, 1, :], lb[:, 2, :], ALU.subtract).then_inc(lb_step, 1)
            c.n += 2
            rows(0)
            dve.wait_ge(lb_act, 1)
            c.link(dve.tensor_tensor(lb[:, 7, :], lb[:, 5, :], lb[:, 6, :], ALU.add))
            c.link(dve.reciprocal(lb[:, 2, :], lb[:, 7, :]))
            c.link(dve.tensor_tensor(lb[:, 0, :], lb[:, 5, :], lb[:, 2, :], ALU.mult))
            dve.tensor_scalar(lb[:, 1, :], lb[:, 0, :], -1.0, 1.0, ALU.mult, ALU.add).then_inc(lb_step, 1)
            lo(0, A0, 0)
            norm(0, A0)
            lo(0, A0, 2)
            lo(0, A0, 3)
            los(A0 + RAW, B0 - A0 - RAW)
            los(B0, RAW)
            dve.wait_ge(col_free, HEADS)
            dve.wait_ge(lb_step, 7)
            for k in range(HEADS):
                m = dve.tensor_scalar(fg[:, k, :], fg[:, k, :], lb[:, 1, k:k + 1], lb[:, 0, k:k + 1], ALU.mult, ALU.add)
            m.then_inc(f_step, 1)
            los(B0 + RAW, RAW)
            dve.wait_ge(f_step, 1)
            dve.tensor_scalar(bsum, fg, TINY, None, ALU.max).then_inc(f_ready, 1)
            los(B0 + 2 * RAW, 4 * RAW)
            dve.wait_ge(mask_in, 48)
            dve.wait_ge(logf_ready, 1)
            for k in range(HEADS):
                m = dve.tensor_tensor_scan(bsum[:, k, :], ones, bsum[:, k, :], 0.0, ALU.mult, ALU.add)
            m.then_inc(b_ready, 1)
            los(B0 + 6 * RAW, D0 - B0 - 6 * RAW)
            lo(0, D0, 0)

            def attention_lo(j):
                k = slice(*ATT_PARTS[j])
                dve.wait_ge(att_hi, j + 1)
                dve.tensor_tensor(xl[:, k, :], att[:, k, :], xh[:, k, :].bitcast(F32), ALU.subtract).then_inc(att_lo, 1)

            soft, mid = Chain(soft_step), Chain(mid_step)
            SOFT, MID = 2, 2

            def d_body(i, u, first=False, last=False):
                hd = 2 * i + u
                lo(2 * i, D0, 4 * u + 1)
                if last:
                    attention_lo(0)
                if not first:
                    soft.start((hd - 1) * SOFT)
                    dve.wait_ge(s_full, hd)
                    soft.link(dve.scalar_tensor_tensor(out=pr, in0=ps[:, 2, 0:3 * P], scalar=-SCALE, in1=cmask,
                                                       op0=ALU.mult, op1=ALU.add))
                    dve.tensor_reduce(small[:, 0:1], pr[:, 0:P], AX, ALU.min)
                    dve.tensor_reduce(small[:, 1:2], pr[:, P:3 * P], AX, ALU.min).then_inc(min_ready, 1)
                if not last:
                    lo(2 * i, D0, 4 * u + 2)
                if not first:
                    dve.wait_ge(exp_ready, 2 * hd)
                    soft.link(dve.reciprocal(small[:, 4:6], small[:, 2:4]))
                    dve.tensor_scalar(pr[:, 0:P], pr[:, 0:P], small[:, 4:5], None, ALU.mult)
                    dve.tensor_scalar(pr[:, P:3 * P], pr[:, P:3 * P], small[:, 5:6], None,
                                      ALU.mult).then_inc(p_ready, 1)
                if not last:
                    lo(2 * i, D0, 4 * u + 3)
                if not first:
                    mid.start((hd - 1) * MID)
                    for t, a in ((0, a00), (1, a11)):
                        dve.wait_ge(a_full, 2 * hd - 1 + t)
                        if not (isinstance(hd, int) and hd == 1 and t == 0):
                            dve.wait_ge(a_ready, 2 * hd - 2 + t)
                        mid.link(dve.tensor_tensor(amask.rearrange("p a b -> p (a b)"),
                                                   ps[:, 3 + 2 * t:5 + 2 * t, :].rearrange("p a b -> p (a b)"),
                                                   masks.rearrange("p a b -> p (a b)"), ALU.mult))
                        r = dve.tensor_reduce(a, amask.rearrange("p l t -> p t l"), AX, ALU.add)
                        r.then_inc(a_ready, 1)
                if not last:
                    lo(2 * i, D0, 4 * u + 4)
                if not last:
                    dve.wait_ge(e_ready, hd + 1)
                    dve.wait_ge(kk_ready, hd + 1)
                    qrow, f = (v[:, bass.DynSlice(hd, 1), :].rearrange("p a b -> p (a b)") for v in (qq, fg))
                    for l in range(NL):
                        ql, kl = halves(QL[:, u * NL + l, :], l), halves(KL[:, u * NL + l, :], l)
                        if l < NL - 1:
                            el = halves(E[:, l, :], l)
                            dve.tensor_tensor(ql[:, :, 1, :], halves(qrow, l)[:, :, 1, :], el[:, :, 1, :], ALU.mult)
                            dve.tensor_tensor(kl[:, :, 0, :], halves(kk[:, u, :], l)[:, :, 0, :], el[:, :, 0, :],
                                              ALU.mult)
                        else:
                            dve.tensor_tensor(ql[:, :, 1, :], halves(qrow, l)[:, :, 1, :], halves(f, l)[:, :, 1, :],
                                              ALU.mult)
                            dve.tensor_copy(kl[:, :, 0, :], halves(kk[:, u, :], l)[:, :, 0, :]).then_inc(qk_ready, 1)

            dve.wait_ge(zeroed, 1)
            d_body(0, 0, first=True)
            d_body(0, 1)
            with dve.Fori(1, HEADS // 2) as i:
                d_body(i, 0)
                d_body(i, 1)
            d_body(HEADS // 2, 0, last=True)
            lo(0, E0, 2)
            attention_lo(1)
            lo(0, E0, 3)
            dve.wait_ge(gain_g, TT)
            dve.wait_ge(r_rs, 1)
            for k in range(HEADS):
                for t in range(TT):
                    o = orec[:, t, k * P:(k + 1) * P]
                    m = dve.scalar_tensor_tensor(out=o, in0=o, scalar=rstd[:, 8 + t * HEADS + k:9 + t * HEADS + k],
                                                 in1=gs[:, t, k * P:(k + 1) * P], op0=ALU.mult, op1=ALU.mult)
                m.then_inc(r_row, 1)
            lo(0, E0, 4)
            for b in range(HEADS // 2):
                if b == 1:
                    lo(0, E0, 5)
                dve.wait_ge(r_hi, b + 1)
                k = slice(HEADS + 2 * b, HEADS + 2 * b + 2)
                dve.tensor_tensor(xl[:, k, :].rearrange("p a b -> p (a b)"), ps[:, R_BANKS[b], :],
                                  xh[:, k, :].rearrange("p a b -> p (a b)").bitcast(F32),
                                  ALU.subtract).then_inc(r_lo, 1)

            def h_add(n):
                dve.wait_ge(tile_done, E0 + (n + 1) * GRPT + HI)
                for t in range(TT):
                    dst = h[:, t, n * GRP:(n + 1) * GRP]
                    dve.tensor_tensor(dst, ps[:, E_BANKS[n] + t, :], dst, ALU.add).then_inc(grp_free, 1)

            for n in range(E_GRPS):
                for s in range(0 if n else GRPT - 2, GRPT):
                    lo(2 * n, E0, s)
                    if n and s == LO - 1:
                        h_add(n - 1)
            h_add(E_GRPS - 1)
            for t in range(TT):
                row_sum(1, t)
            rows(1)
            lo(0, F0, 0)
            norm(1, F0)
            lo(0, F0, 2)
            lo(0, F0, 3)
            los(F0 + RAW, G0 - F0 - RAW)

            rt = Chain(rt_step)
            ROUTE = 13

            def hold(k):
                dve.memset(small[:, k:k + 1], 0.0)

            def route(r):
                def split(s):
                    lo(ROUTE_TILES // RAW * r, G0, s)

                rt.start(r * ROUTE)
                split(0)
                dve.wait_ge(sc_sb, 8)
                dve.wait_ge(routed, r)
                rt.mark(dve.tensor_scalar(sg, sc[:, bass.DynSlice(2 * r, 2), :], 1.0, None, ALU.mult))
                split(1)
                rt.sync()
                hold(0)
                for k in range(2):
                    m = dve.max(top[:, k, 0:8], sg[:, k, :])
                rt.mark(m)
                rt.sync()
                hold(1)
                for k in range(2):
                    dve.max_index(tixu[:, k, 0:8], top[:, k, 0:8], sg[:, k, :])
                    m = dve.match_replace(sg2[:, k, :], top[:, k, 0:8], sg[:, k, :], NEG)
                rt.mark(m)
                split(2)
                rt.sync()
                hold(2)
                for k in range(2):
                    m = dve.max(top[:, k, 8:TOP], sg2[:, k, :])
                rt.mark(m)
                rt.sync()
                hold(3)
                for k in range(2):
                    dve.max_index(tixu[:, k, 8:TOP], top[:, k, 8:TOP], sg2[:, k, :])
                rt.mark(dve.tensor_tensor(cand, top[:, 0, :].unsqueeze(2).to_broadcast([P, TOP, TOP]),
                                          top[:, 1, :].unsqueeze(1).to_broadcast([P, TOP, TOP]), ALU.add))
                split(3)
                rt.sync()
                cf, cf2 = (v.rearrange("p a b -> p (a b)") for v in (cand, cand2))
                dve.tensor_copy(tix, tixu)
                rt.mark(dve.max(bst[:, 0:8], cf))
                rt.sync()
                hold(4)
                dve.max_index(posu[:, 0:8], bst[:, 0:8], cf)
                rt.mark(dve.match_replace(cf2, bst[:, 0:8], cf, NEG))
                split(4)
                rt.sync()
                hold(5)
                rt.mark(dve.max(bst[:, 8:TOP], cf2))
                rt.sync()
                hold(6)
                rt.mark(dve.max_index(posu[:, 8:TOP], bst[:, 8:TOP], cf2))
                split(5)
                rt.sync()
                dve.tensor_scalar(best[:, r, :], bst, bst[:, 0:1], None, ALU.subtract)
                dve.tensor_scalar(abu[:, 0, :], posu, 4, None, ALU.logical_shift_right)
                rt.mark(dve.tensor_scalar(abu[:, 1, :], posu, TOP - 1, None, ALU.bitwise_and))
                rt.sync()
                rt.mark(dve.tensor_copy(ab, abu))
                split(6)
                rt.sync()
                ohf = oh.rearrange("p a b c -> p (a b) c")
                rt.mark(dve.tensor_tensor(ohf,
                                          ab.rearrange("p a b -> p (a b)").unsqueeze(2).to_broadcast([P, 2 * TOP, TOP]),
                                          iota[:, 0:TOP].unsqueeze(1).to_broadcast([P, 2 * TOP, TOP]), ALU.is_equal))
                split(7)
                rt.sync()
                for k in range(2):
                    m = dve.tensor_tensor(oh[:, k, :, :], oh[:, k, :, :],
                                          tix[:, k, :].unsqueeze(1).to_broadcast([P, TOP, TOP]), ALU.mult)
                rt.mark(m)
                rt.sync()
                assert rt.n == ROUTE
                dve.tensor_reduce(i1[:, r, :], oh[:, 0, :, :], AX, ALU.add)
                dve.tensor_reduce(i2[:, r, :], oh[:, 1, :, :], AX, ALU.add).then_inc(routed, 1)

            with dve.Fori(0, TT * PH) as r:
                route(r)
            lo(GT0, G0, 0)
            lo(GT0, G0, 1)
            gc = Chain(g_step)
            dve.wait_ge(gexp, 1)
            gc.link(dve.tensor_reduce(gsum, best, AX, ALU.add))
            gc.link(dve.reciprocal(gsum, gsum))
            dve.tensor_tensor(gate, best, gsum.unsqueeze(2).to_broadcast([P, TT * PH, TOP]),
                              ALU.mult).then_inc(gates, 1)
            lo(GT0, G0, 2)
            lo(GT0, G0, 3)

            def onehots(g, u):
                tk = slice(GATED * u, GATED * (u + 1))
                dve.tensor_tensor(oneL[:, tk, :],
                                  slotT[:, 0, bass.DynSlice(GATED * g, GATED)].unsqueeze(2).to_broadcast([P, GATED, P]),
                                  iota.unsqueeze(1).to_broadcast([P, GATED, P]), ALU.is_equal)
                for t in range(GATED):
                    m = dve.tensor_scalar(gateR[:, GATED * u + t, :], iota,
                                          slotT[:, 1, bass.DynSlice(GATED * g + t, 1)],
                                          slotT[:, 2, bass.DynSlice(GATED * g + t, 1)], ALU.is_equal, ALU.mult)
                m.then_inc(oh_ready, 1)

            def apply(g, u):
                dve.wait_ge(g_pre, g + 1)
                dst = coef_t[:, bass.DynSlice(GATED * g, GATED), 0:DIRECT]
                dve.tensor_tensor(dst, dst, ps[:, 5 + u, :].rearrange("p (t e) -> p t e", t=GATED)[:, :, 0:DIRECT],
                                  ALU.mult).then_inc(gm_mul, 1)

            def gate_trip(k, first=False):
                j = k + (GT0 + 1)
                lo(j, G0, 0)
                if first:
                    apply(0, 0)
                onehots(2 * k, 0)
                lo(j, G0, 1)
                apply(2 * k - 1, 1)
                lo(j, G0, 2)
                onehots(2 * k + 1, 1)
                lo(j, G0, 3)
                apply(2 * k, 0)

            for s in range(RAW):
                lo(GT0 + 1, G0, s)
            dve.wait_ge(it_sb, 3)
            onehots(0, 0)
            onehots(1, 1)
            gate_trip(1, True)
            with dve.Fori(2, GTRIPS) as k:
                gate_trip(k)
            lo(0, U0, 0)
            for g in range(2 * GTRIPS, S // GATED):
                onehots(g, g % 2)
                apply(g - 1, (g - 1) % 2)
            lo(0, U0, 1)
            apply(S // GATED - 1, 1)

            def multiply(m, v):
                dve.wait_ge(st_in[v], 8 * m + (16 - 8 * v))
                dst = coef[:, bass.DynSlice(m + DIRECT, 1), :].rearrange("p a b -> p (a b)")
                dve.tensor_tensor(dst, dst, stage[:, v, :], ALU.mult).then_inc(c_mul, 1)

            def u_body(i, first=False, back=False, last=False):
                for v in range(2):
                    if not (first and v == 0):
                        lo(i, U0, 2 * v)
                    if back and not (last and v == 1):
                        multiply(2 * i + (v + 1 - DIRECT), 1 - v)
                    dve.wait_ge(c_hi, 2 * i + (v + 1))
                    dve.tensor_tensor(cl[:, v, :], coef[:, 2 * i + v, :], ch[:, v, :].bitcast(F32),
                                      ALU.subtract).then_inc(c_lo, 1)
                    if not (first and v == 0):
                        lo(i, U0, 2 * v + 1)

            u_body(0, first=True)
            with dve.Fori(1, GT0) as i:
                u_body(i)
            multiply(0, 0)
            with dve.Fori(GT0, NK // 2 - 1) as i:
                u_body(i, back=True)
            u_body(NK // 2 - 1, back=True, last=True)
            dve.wait_ge(h_back, 16 * TT)
            for t in range(TT):
                if t == 0:
                    dve.wait_ge(u_first, 1)
                else:
                    dve.wait_ge(tile_done, W0 + HI)
                for g in range(4):
                    dst = h[:, t, g * GRP:(g + 1) * GRP]
                    dve.tensor_tensor(dst, ps[:, 4 * t + g, :], dst, ALU.add).then_inc(h_up, 1)
                    if t == 1 and g == 0:
                        row_sum(2, 0)
            row_sum(2, 1)
            rows(2)
            lo(0, W0, 0)
            norm(2, W0)

            def w_out(g):
                j = g % 2
                c = slice(g * GRP, (g + 1) * GRP)
                for t in range(TT):
                    n = TT * g + t
                    dve.wait_ge(w_sig, n + 1)
                    dve.tensor_tensor(ple_m[:, 2 * j + t, :], ps[:, 6 * j + t, :],
                                      sgate[:, 2 * j + t, :], ALU.mult).then_inc(grp_free, 1)
                    dve.wait_ge(grp_free, TT * GW + n + 1)
                    dve.tensor_tensor(h[:, t, c], ple_m[:, 2 * j + t, :], h[:, t, c], ALU.add).then_inc(w_add, 1)
                for t in range(TT):
                    dve.wait_ge(w_add, TT * g + t + 1)
                    dve.tensor_tensor(orow[:, t, c], h[:, t, c], gf_row[:, c], ALU.mult).then_inc(f_gain, 1)

            dve.wait_ge(ple_in, 16 * (PK + 2))
            for n in range(W_GRPS):
                for s in range(GRPT):
                    if n or s >= LO:
                        lo(2 * n, W0, s)
                    if n and s == HI - 1:
                        w_out(n - 1)
            w_out(W_GRPS - 1)
            for t in range(TT):
                row_sum(3, t)
            dve.wait_ge(n_rs[3], 1)
            dve.wait_ge(f_gain, TT * W_GRPS)
            for c in range(2):
                o = orow[:, 0, c * D // 2:(c + 1) * D // 2]
                dve.tensor_scalar(o, o, rstd[:, 6:7], None, ALU.mult).then_inc(f_row[0], 1)

        @block.tensor
        def _(pe):
            def norm(k):
                for c in range(KC):
                    if c % (KC // 2) == 0:
                        pe.wait_ge(n_row0[k], c // (KC // 2) + 1)
                        pe.wait_ge(n_row1[k], c // (KC // 2) + 1)
                    if k == 0 and c == 0:
                        pe.wait_ge(const_in, 48)
                    for t in range(TT):
                        mm = pe.transpose(ps[:, c // 2, (c % 2) * S + t * P:(c % 2) * S + (t + 1) * P],
                                          hn[:, t, c * P:(c + 1) * P], ident)
                    if c % 2:
                        mm.then_inc(n_tr[k], 1)
                pe.wait_ge(n_xl[k], KC // 4)

            def parts(s, width):
                return (w.rearrange("p (k c) -> p k c", c=width) for w in (whi[:, s % HI, :], wlo[:, s % LO, :]))

            def col_tile(i, base, s, bank, second, free=None):
                if free is not None:
                    pe.wait_ge(col_free, free)
                pe.wait_ge(lo_ready, RAW * i + (base + s + 1))
                wh, wl = parts(s, P)
                for k in range(KPC):
                    kc = second * KPC + k
                    pe.matmul(col_ps(bank), wh[:, k, :], xh[:, kc, :], start=(kc == 0), stop=False)
                    pe.matmul(col_ps(bank), wh[:, k, :], xl[:, kc, :], start=False, stop=False)
                    mm = pe.matmul(col_ps(bank), wl[:, k, :], xh[:, kc, :], start=False, stop=(kc == KC - 1))
                mm.then_inc(tile_done, 1)

            def cols(base, c0, trips, after=None):
                def body(i, free, norm_=None):
                    for s in range(RAW):
                        if norm_ is not None and s == 1:
                            pe.wait_ge(n_xl[norm_], KC // 2)
                        col_tile(i, base, s, s // COLT, s % COLT,
                                 2 * i + (c0 + s // COLT - 1) if free and s % COLT == 0 else None)

                if after is not None:
                    body(0, c0 > 0, after)
                with pe.Fori(0 if after is None else 1, trips) as i:
                    body(i, True)

            def grp_tile(i, base, s, kt, bank):
                pe.wait_ge(lo_ready, RAW * i + (base + s + 1))
                wh, wl = parts(s, GRP)
                for t in range(TT):
                    tk = slice(t * P, (t + 1) * P)
                    for k in range(KPG):
                        kc = kt * KPG + k
                        o = ps[:, bank + t, :]
                        pe.matmul(o, xh[:, kc, tk], wh[:, k, :], start=(kc == 0), stop=False)
                        pe.matmul(o, xl[:, kc, tk], wh[:, k, :], start=False, stop=False)
                        mm = pe.matmul(o, xh[:, kc, tk], wl[:, k, :], start=False, stop=(kc == KC - 1))
                mm.then_inc(tile_done, 1)

            def groups(base, g0, pairs, start=0, first=False, after=None, extra=None):
                def body(i, free, norm_=None):
                    for j in range(2):
                        if free:
                            pe.wait_ge(grp_free, TT * 2 * i + TT * (g0 + j - 1))
                        for s in range(GRPT):
                            if s == GRPT // 2:
                                if norm_ is not None and j == 0:
                                    pe.wait_ge(n_xl[norm_], KC // 2)
                                if extra is not None:
                                    extra(i, j)
                            grp_tile(4 * i, base, j * GRPT + s, s, 2 + 2 * j)

                if first or after is not None:
                    body(0, not first, after)
                    start = 1
                with pe.Fori(start, pairs) as i:
                    body(i, True)

            pe.sem_inc(tile_done, HI)
            norm(0)
            cols(A0, CA, A_COLS // 2, after=0)
            groups(B0, GB, B_GRPS // 2, first=True)

            def e_wait(s):
                if s < GRPT // 2:
                    pe.wait_ge(att_lo, 1 if 2 * s < ATT_PARTS[0][1] else 2)
                else:
                    pe.wait_ge(r_lo, s - GRPT // 2 + 1)

            E_EARLY = 2

            def d_body(i, u, first=False, last=False):
                hd = 2 * i + u
                v = 1 - u
                if not last:
                    col_tile(2 * i, D0, 4 * u, 0, 0, 2 * hd + (CD - 1))
                if not first:
                    pe.wait_ge(col_free, 2 * hd + CD)
                    if isinstance(hd, int) and hd == 1:
                        pe.wait_ge(grp_free, TT * B_GRPS)
                    else:
                        pe.wait_ge(att_sb, hd - 1)
                    q, k = qk[:, 2 * v, :], qk[:, 2 * v + 1, :]
                    pe.matmul(ps[:, 2, 0:P], q[:, 0:P], k[:, 0:P], start=True, stop=True)
                    pe.matmul(ps[:, 2, P:3 * P], q[:, P:S], k, start=True, stop=True).then_inc(s_full, 1)
                if not last:
                    col_tile(2 * i, D0, 4 * u + 1, 0, 1)
                if not first:
                    pe.wait_ge(qk_ready, hd)
                    if not (isinstance(hd, int) and hd == 1):
                        pe.wait_ge(rec_sb, 2 * hd - 2)
                    for t in range(TT):
                        tk = slice(t * P, (t + 1) * P)
                        if t == 0:
                            pe.matmul(ps[:, 7, 3 * P:4 * P], KL[:, v * NL, 0:P], QL[:, v * NL, P:S],
                                      start=True, stop=True)
                        for l in range(1, NL + 1):
                            o = ps[:, 3 + 2 * t + (l - 1) // 4, (l - 1) % 4 * P:((l - 1) % 4 + 1) * P]
                            if l < NL:
                                pe.matmul(o, KL[:, v * NL + l, tk], QL[:, v * NL + l, tk], start=True, stop=True)
                            else:
                                qd = qq[:, bass.DynSlice(hd - 1, 1), tk].rearrange("p a b -> p (a b)")
                                mm = pe.matmul(o, kk[:, v, tk], qd, start=True, stop=True)
                        mm.then_inc(a_full, 1)
                if not last:
                    col_tile(2 * i, D0, 4 * u + 2, 1, 0, 2 * hd + CD)
                else:
                    e_wait(0)
                    grp_tile(0, E0, 0, 0, E_BANKS[0])
                if not first:
                    pe.wait_ge(ax_ready, hd)
                    pe.wait_ge(p_ready, hd)
                    for j in range(3):
                        mm = pe.transpose(ps[:, 7, j * P:(j + 1) * P], pr[:, j * P:(j + 1) * P], ident)
                    mm.then_inc(pt_full, 1)
                if not last:
                    col_tile(2 * i, D0, 4 * u + 3, 1, 1)
                else:
                    e_wait(1)
                    grp_tile(0, E0, 1, 1, E_BANKS[0])
                if not first:
                    pe.wait_ge(pt_sb, hd)
                    pe.wait_ge(v_ready, hd)
                    pe.matmul(ps[:, 2, 0:P], vh[:, 0, :], pT[:, 0:P], start=True, stop=True)
                    pe.matmul(ps[:, 2, P:S], vh[:, 0, :], pT[:, P:S], start=True, stop=False)
                    pe.matmul(ps[:, 2, P:S], vh[:, 1, :], pT[:, S:3 * P], start=False, stop=True)
                    pe.wait_ge(a_ready, 2 * hd)
                    vr = [gi[:, t, bass.DynSlice((hd - 1) * P, P)] for t in range(TT)]
                    pe.matmul(ps[:, 3, 0:P], a00, vr[0], start=True, stop=True)
                    pe.matmul(ps[:, 3, P:S], a01, vr[0], start=True, stop=False)
                    pe.matmul(ps[:, 3, P:S], a11, vr[1], start=False, stop=True).then_inc(o_full, 1)

            d_body(0, 0, first=True)
            d_body(0, 1)
            with pe.Fori(1, HEADS // 2) as i:
                d_body(i, 0)
                d_body(i, 1)
            d_body(HEADS // 2, 0, last=True)

            for n in range(E_GRPS):
                for s in range(E_EARLY if n == 0 else 0, GRPT):
                    if n == 0 and s == GRPT // 2:
                        pe.wait_ge(rec_sb, 2 * HEADS)
                        for c in range(HEADS):
                            pe.wait_ge(r_row, c + 1)
                            for t in range(TT):
                                mm = pe.transpose(ps[:, R_BANKS[c // 2],
                                                     (c % 2) * S + t * P:(c % 2) * S + (t + 1) * P],
                                                  orec[:, t, c * P:(c + 1) * P], ident)
                            if c % 2:
                                mm.then_inc(r_tr, 1)
                    if n == 0:
                        e_wait(s)
                    elif s == 0 and n >= 2:
                        pe.wait_ge(grp_free, TT * (GE + n - 1))
                    grp_tile(2 * n, E0, s, s, E_BANKS[n])
            norm(1)
            cols(F0, CF, PH, after=1)
            pe.wait_ge(sk_in, 16)
            pe.wait_ge(col_free, CG)
            for t in range(TT):
                for g in range(2 * PH):
                    n = t * 2 * PH + g
                    mm = pe.matmul(ps[:, n // 4, n % 4 * P:(n % 4 + 1) * P], qT[:, g, t * P:(t + 1) * P],
                                   sk[:, g, :], start=True, stop=True)
                    if n % 4 == 3:
                        mm.then_inc(sc_full, 1)
            pe.wait_ge(sc_sb, 2)
            cols(G0, CG, GT0 + 1)
            pe.wait_ge(gates, 1)
            pe.wait_ge(sc_sb, 8)
            for j, v in enumerate((i1, i2, gate)):
                flat = v.rearrange("p a b -> p (a b)")
                for t in range(TT):
                    mm = pe.transpose(ps[:, 2 + j, t * P:(t + 1) * P], flat[:, t * P:(t + 1) * P], ident)
                mm.then_inc(it_full, 1)

            def gate_products(g, u, first):
                pe.wait_ge(oh_ready, g + 1)
                if not first:
                    pe.wait_ge(gm_mul, g - 1)
                for t in range(GATED):
                    mm = pe.matmul(ps[:, 5 + u, t * P:(t + 1) * P], oneL[:, GATED * u + t, :],
                                   gateR[:, GATED * u + t, :], start=True, stop=True)
                mm.then_inc(gm_full, 1)

            def gate_trip(k):
                j = k + (GT0 + 1)
                first = isinstance(k, int) and k == 0
                for s in range(RAW):
                    col_tile(j, G0, s, s // COLT, s % COLT, 2 * j + (CG + s // COLT - 1) if s % COLT == 0 else None)
                    if s % COLT and not first:
                        gate_products(2 * k + s // COLT, s // COLT, False)
                if first:
                    for u in range(2):
                        gate_products(u, u, True)

            gate_trip(0)
            with pe.Fori(1, GTRIPS) as k:
                gate_trip(k)
            for g in range(2 * GTRIPS, S // GATED):
                gate_products(g, g % 2, False)

            def up_products(s, v, t, first, last):
                wh, wl = parts(s, GRP)
                tk = slice(t * P, (t + 1) * P)
                for k in range(KPG):
                    o = ps[:, 4 * t + 2 * (s % 2) + k, :]
                    pe.matmul(o, ch[:, v, tk], wh[:, k, :], start=first, stop=False)
                    pe.matmul(o, cl[:, v, tk], wh[:, k, :], start=False, stop=False)
                    mm = pe.matmul(o, ch[:, v, tk], wl[:, k, :], start=False, stop=last)
                return mm

            def u_body(i, first=False, last=False):
                for s in range(RAW // 2 if last else RAW):
                    v = s // COLT
                    if s % COLT == 0:
                        pe.wait_ge(c_lo, 2 * i + (v + 1))
                    pe.wait_ge(lo_ready, RAW * i + (U0 + s + 1))
                    for t in range(TT):
                        mm = up_products(s, v, t, first and v == 0, False)
                    mm.then_inc(tile_done, 1)

            def u_last():
                pe.wait_ge(c_lo, NK)
                for t in range(TT):
                    for s in range(RAW - COLT, RAW):
                        if t == 0:
                            pe.wait_ge(lo_ready, W0 - RAW + s + 1)
                        mm = up_products(s, 1, t, False, True)
                        if t == TT - 1:
                            mm.then_inc(tile_done, 1)
                    if t == 0:
                        mm.then_inc(u_first, 1)

            u_body(0, first=True)
            with pe.Fori(1, NK // 2 - 1) as i:
                u_body(i)
            u_body(NK // 2 - 1, last=True)
            u_last()
            norm(2)

            def embed(i, j):
                for t in range(TT):
                    for k in range(PK):
                        pe.matmul(ps[:, 6 * j + t, :], ple_p[:, k, t * P:(t + 1) * P],
                                  ple_w[:, k, bass.DynSlice(i * (2 * GRP) + j * GRP, GRP)],
                                  start=(k == 0), stop=(k == PK - 1))

            pe.wait_ge(ple_in, 16 * (PK + 2))
            groups(W0, GW, W_GRPS // 2, after=2, extra=embed)


_OUT = ((1, S, D), "float32")


def blocks_of_columns(w):
    n = w.shape[1] // P
    return w.reshape(COLT, KPC, P, n, P).transpose(3, 0, 2, 1, 4).reshape(n * COLT, P, TILE)


def groups_of_columns(w):
    n = w.shape[1] // GRP
    return w.reshape(GRPT, KPG, P, n, GRP).transpose(3, 0, 2, 1, 4).reshape(n * GRPT, P, TILE)


def kernel(x, p, norm_mix, w_in, lb_logits, hgrn_norm, w_out, norm_ffn, peer_query, peer_sub_keys, peer_down,
           peer_up, norm_ple, w_ple, w_ple_gate, norm_final):
    import concourse.bacc as bacc
    from concourse.bass_utils import run_bass_kernel_spmd

    x, p, w_in, w_out, wq, wg = (np.asarray(a) for a in (x, p, w_in, w_out, peer_query, w_ple_gate))
    aq, ak, av, gq, gf, gi, gg = (w_in[0][:, k * HW:(k + 1) * HW] for k in range(7))
    heads = [a[:, k * P:(k + 1) * P] for k in range(HEADS) for a in (aq, ak)]
    rows = np.arange(P)
    s, t = rows[:, None], rows[None, :]
    level = [(s // (2 * m) == t // (2 * m)) & (s % (2 * m) < m) & (t % (2 * m) >= m) for m in HALVES[1:]]
    level_masks = np.stack(level + [s == t], 1).reshape(P, NL * P).astype(np.float32)
    hide = np.where(t > s, np.float32(-NEG), np.float32(0))
    consts = np.concatenate([np.eye(P), np.tile(rows, (P, 1))], 1).astype(np.float32)
    mix_consts = np.concatenate([hide, np.zeros((P, P)), hide, np.ones((P, S))], 1).astype(np.float32)
    gains = np.stack([np.asarray(g).reshape(KC, P).T for g in (norm_mix, norm_ffn, norm_ple)], 1)
    arrays = {
        "x": x.reshape(S, D),
        "win_t": blocks_of_columns(np.concatenate([gf, gq] + heads, 1)),
        "win_n": groups_of_columns(np.concatenate([gi, gg, av], 1)),
        "wout": groups_of_columns(w_out[0]),
        "wq": blocks_of_columns(wq[0]),
        "down": np.asarray(peer_down).reshape(NK, NK, COLT, KPC, P).transpose(1, 2, 4, 3, 0).reshape(-1, P, TILE),
        "up": np.asarray(peer_up).reshape(NK, NK, D),
        "wgate": groups_of_columns(wg[0]),
        "gains": gains,
        "lbl": np.asarray(lb_logits).reshape(2, HEADS, P).transpose(2, 0, 1),
        "gain_h": np.asarray(hgrn_norm).reshape(HW),
        "gain_f": np.asarray(norm_final).reshape(D),
        "skt": np.asarray(peer_sub_keys).reshape(2 * PH, NK, P).transpose(2, 0, 1).reshape(P, 2 * PH * NK),
        "pt": p.reshape(S, PK, P).transpose(2, 1, 0),
        "wple": np.asarray(w_ple).reshape(PK, P, D).transpose(1, 0, 2),
        "consts": consts,
        "mix_consts": mix_consts,
        "level_masks": level_masks,
    }
    arrays = {f"in_{k}": np.ascontiguousarray(v) for k, v in arrays.items()}
    nc = bacc.Bacc("TRN2", target_bir_lowering=False, num_devices=1, dynamic_dma_scratch_size=1024)
    ins = {k: nc.dram_tensor(k, a.shape, mybir.dt.from_np(a.dtype), kind="ExternalInput").ap()
           for k, a in arrays.items()}
    o = nc.dram_tensor("out_0", [S, D], F32, kind="ExternalOutput").ap()
    ins["in_up"] = ins["in_up"].rearrange("a b d -> b a d")
    program(nc, out=o, **{k[3:]: v for k, v in ins.items()})
    r = run_bass_kernel_spmd(nc, [arrays], core_ids=[0])
    return r.results[0]["out_0"].reshape(_OUT[0])
```
